# Optimizing a Trainium2 kernel written in Bass

```python
import math
import jax, jax.numpy as jnp
from jax import lax
import numpy as np

D_MODEL = 1024
BATCH = 1
SEQ = 512
DEPTH = 2

CHUNK = 64
N_A_LAYERS = DEPTH // 2
N_B_LAYERS = DEPTH - N_A_LAYERS

A_HEADS = 8
A_HEAD_K = 128
A_HEAD_V = 128
A_QK_WIDTH = A_HEADS * A_HEAD_K
A_V_WIDTH = A_HEADS * A_HEAD_V
A_CONV = 4
A_CONV_WIDTH = 2 * A_QK_WIDTH + A_V_WIDTH
A_IN_WIDTH = 2 * A_QK_WIDTH + 2 * A_V_WIDTH + 2 * A_HEADS

B_HEADS = 16
B_HEAD_DIM = 64
B_WIDTH = B_HEADS * B_HEAD_DIM
LEFT_CHUNKS = 8
BAND = (LEFT_CHUNKS + 1) * CHUNK
REL_CLIP = 256

FFN_DIM = 2816
FFN_CONV = 3

EPS = 1e-6
NEG_INF = -1e30


def rmsnorm(x, g):
    xf = x.astype(jnp.float32)
    y = xf * lax.rsqrt(jnp.mean(xf * xf, axis=-1, keepdims=True) + EPS)
    return (y * g.astype(jnp.float32)).astype(x.dtype)

def causal_dwconv(x, w):
    width = w.shape[0]
    return lax.conv_general_dilated(
        x, w[:, None, :].astype(x.dtype), window_strides=(1,), padding=[(width - 1, 0)],
        dimension_numbers=("NWC", "WIO", "NWC"), feature_group_count=x.shape[-1])

def _l2norm(t):
    return t * lax.rsqrt(jnp.sum(t * t, axis=-1, keepdims=True) + EPS)

def chunk_gated_delta_rule(q, k, v, beta, g):
    bsz, seq, nh, dk = q.shape
    dv = v.shape[-1]
    nc = seq // CHUNK

    def chunks(t):
        return t.reshape(bsz, nc, CHUNK, nh, -1).transpose(0, 3, 1, 2, 4)

    q, k, v = chunks(q), chunks(k), chunks(v)
    beta = chunks(beta[..., None])[..., 0]
    gcum = jnp.cumsum(chunks(g[..., None])[..., 0], axis=-1)

    causal = jnp.tril(jnp.ones((CHUNK, CHUNK), dtype=bool))
    strict = jnp.tril(jnp.ones((CHUNK, CHUNK), dtype=bool), k=-1)
    diff = gcum[..., :, None] - gcum[..., None, :]
    decay = jnp.where(causal, jnp.exp(jnp.where(causal, diff, 0.0)), 0.0)

    k_beta = k * beta[..., None]
    m = jnp.where(strict, jnp.einsum("bhnid,bhnjd->bhnij", k_beta, k) * decay, 0.0)
    eye = jnp.eye(CHUNK, dtype=m.dtype)
    rhs = jnp.concatenate([v * beta[..., None], k_beta * jnp.exp(gcum)[..., None]], axis=-1)
    uw = lax.linalg.triangular_solve(m + eye, rhs, left_side=True, lower=True, unit_diagonal=True)
    u, w = uw[..., :dv], uw[..., dv:]

    attn_qk = jnp.einsum("bhnid,bhnjd->bhnij", q, k) * decay
    q_dec = q * jnp.exp(gcum)[..., None]
    k_end = k * jnp.exp(gcum[..., -1:] - gcum)[..., None]
    chunk_decay = jnp.exp(gcum[..., -1])

    xs = tuple(jnp.moveaxis(t, 2, 0) for t in (q_dec, k_end, u, w, attn_qk, chunk_decay))

    def step(state, inp):
        qd, ke, u_c, w_c, a_c, dec = inp
        v_new = u_c - jnp.einsum("bhcd,bhdv->bhcv", w_c, state)
        o_c = jnp.einsum("bhcd,bhdv->bhcv", qd, state) + jnp.einsum("bhcj,bhjv->bhcv", a_c, v_new)
        state = state * dec[..., None, None] + jnp.einsum("bhcd,bhcv->bhdv", ke, v_new)
        return state, o_c

    state0 = jnp.zeros((bsz, nh, dk, dv), jnp.float32)
    _, o = lax.scan(step, state0, xs)
    return o.transpose(1, 0, 3, 2, 4).reshape(bsz, seq, nh, dv)

def gated_deltanet(xn, w_in, conv_w, A_log, dt_bias, out_norm_w, w_out):
    bsz, seq, _ = xn.shape
    proj = xn @ w_in
    qkv = jax.nn.silu(causal_dwconv(proj[..., :A_CONV_WIDTH], conv_w))
    z = proj[..., A_CONV_WIDTH:A_CONV_WIDTH + A_V_WIDTH]
    b_raw = proj[..., A_CONV_WIDTH + A_V_WIDTH:A_CONV_WIDTH + A_V_WIDTH + A_HEADS]
    a_raw = proj[..., A_CONV_WIDTH + A_V_WIDTH + A_HEADS:]
    f32 = jnp.float32
    q = _l2norm(qkv[..., :A_QK_WIDTH].reshape(bsz, seq, A_HEADS, A_HEAD_K).astype(f32)) * (A_HEAD_K ** -0.5)
    k = _l2norm(qkv[..., A_QK_WIDTH:2 * A_QK_WIDTH].reshape(bsz, seq, A_HEADS, A_HEAD_K).astype(f32))
    v = qkv[..., 2 * A_QK_WIDTH:].reshape(bsz, seq, A_HEADS, A_HEAD_V).astype(f32)
    beta = jax.nn.sigmoid(b_raw.astype(f32))
    g = -jnp.exp(A_log.astype(f32)) * jax.nn.softplus(a_raw.astype(f32) + dt_bias.astype(f32))
    o = chunk_gated_delta_rule(q, k, v, beta, g).astype(xn.dtype)
    o = rmsnorm(o, out_norm_w) * jax.nn.silu(z.reshape(bsz, seq, A_HEADS, A_HEAD_V))
    return o.reshape(bsz, seq, A_V_WIDTH) @ w_out

def chunk_attention(xn, w_q, rel_bias, w_out, k_pad, v_pad):
    bsz, seq, _ = xn.shape
    nc = seq // CHUNK
    q = (xn @ w_q).reshape(bsz, nc, CHUNK, B_HEADS, B_HEAD_DIM).transpose(1, 0, 2, 3, 4)
    rel = jnp.arange(CHUNK)[:, None] + LEFT_CHUNKS * CHUNK - jnp.arange(BAND)[None, :]
    bias = rel_bias[:, jnp.clip(rel, -REL_CLIP, REL_CLIP) + REL_CLIP].astype(jnp.float32)
    scale = B_HEAD_DIM ** -0.5

    def one_chunk(args):
        n, q_n = args
        k_band = lax.dynamic_slice_in_dim(k_pad, n * CHUNK, BAND, axis=1)
        v_band = lax.dynamic_slice_in_dim(v_pad, n * CHUNK, BAND, axis=1)
        s = jnp.einsum("bqhd,bkhd->bhqk", q_n, k_band).astype(jnp.float32) * scale + bias
        valid = jnp.arange(BAND) >= (LEFT_CHUNKS - n) * CHUNK
        s = jnp.where(valid, s, NEG_INF)
        p = jax.nn.softmax(s, axis=-1).astype(v_band.dtype)
        return jnp.einsum("bhqk,bkhd->bqhd", p, v_band)

    o = lax.map(one_chunk, (jnp.arange(nc, dtype=jnp.int32), q))
    o = o.transpose(1, 0, 2, 3, 4).reshape(bsz, seq, B_WIDTH)
    return o @ w_out

def conv_ffn(xn, w_up, conv_w, conv_b, w_down):
    h = causal_dwconv(xn @ w_up, conv_w) + conv_b
    gate, val = h[..., :FFN_DIM], h[..., FFN_DIM:]
    return (jax.nn.silu(gate) * val) @ w_down

def first_inputs(seed: int = 0) -> dict:
    key = jax.random.key(seed)
    ks = jax.random.split(key, 22)

    def nrm(k, shape, scale):
        return jax.random.normal(k, shape, jnp.float32) * scale

    dt = jnp.exp(jax.random.uniform(ks[5], (N_A_LAYERS, A_HEADS), jnp.float32,
                                    minval=math.log(1e-3), maxval=math.log(1e-1)))
    return {
        "x": nrm(ks[0], (BATCH, SEQ, D_MODEL), 1.0),
        "a_norm": 1.0 + nrm(ks[1], (N_A_LAYERS, D_MODEL), 0.02),
        "a_w_in": nrm(ks[2], (N_A_LAYERS, D_MODEL, A_IN_WIDTH), D_MODEL ** -0.5),
        "a_conv": nrm(ks[3], (N_A_LAYERS, A_CONV, A_CONV_WIDTH), A_CONV ** -0.5),
        "a_A_log": jnp.log(jax.random.uniform(ks[4], (N_A_LAYERS, A_HEADS), jnp.float32, minval=1.0, maxval=16.0)),
        "a_dt_bias": dt + jnp.log(-jnp.expm1(-dt)),
        "a_out_norm": 1.0 + nrm(ks[6], (N_A_LAYERS, A_HEAD_V), 0.02),
        "a_w_out": nrm(ks[7], (N_A_LAYERS, A_V_WIDTH, D_MODEL), A_V_WIDTH ** -0.5),
        "kv_norm": 1.0 + nrm(ks[8], (D_MODEL,), 0.02),
        "w_kv": nrm(ks[9], (D_MODEL, 2 * B_WIDTH), D_MODEL ** -0.5),
        "b_norm": 1.0 + nrm(ks[10], (N_B_LAYERS, D_MODEL), 0.02),
        "b_w_q": nrm(ks[11], (N_B_LAYERS, D_MODEL, B_WIDTH), D_MODEL ** -0.5),
        "b_rel_bias": nrm(ks[12], (N_B_LAYERS, B_HEADS, 2 * REL_CLIP + 1), 0.1),
        "b_w_out": nrm(ks[13], (N_B_LAYERS, B_WIDTH, D_MODEL), B_WIDTH ** -0.5),
        "f_norm": 1.0 + nrm(ks[14], (DEPTH, D_MODEL), 0.02),
        "f_w_up": nrm(ks[15], (DEPTH, D_MODEL, 2 * FFN_DIM), D_MODEL ** -0.5),
        "f_conv": nrm(ks[16], (DEPTH, FFN_CONV, 2 * FFN_DIM), FFN_CONV ** -0.5),
        "f_conv_b": nrm(ks[17], (DEPTH, 2 * FFN_DIM), 0.01),
        "f_w_down": nrm(ks[18], (DEPTH, FFN_DIM, D_MODEL), FFN_DIM ** -0.5),
        "final_norm": 1.0 + nrm(ks[19], (D_MODEL,), 0.02),
    }

def first_block(x, a_norm, a_w_in, a_conv, a_A_log, a_dt_bias, a_out_norm, a_w_out,
              kv_norm, w_kv, b_norm, b_w_q, b_rel_bias, b_w_out,
              f_norm, f_w_up, f_conv, f_conv_b, f_w_down, final_norm):
    bsz, seq, _ = x.shape
    h = x
    k_pad = None
    v_pad = None
    for layer in range(DEPTH):
        if layer < N_A_LAYERS:
            i = layer
            h = h + gated_deltanet(rmsnorm(h, a_norm[i]), a_w_in[i], a_conv[i], a_A_log[i],
                                   a_dt_bias[i], a_out_norm[i], a_w_out[i])
        else:
            if layer == N_A_LAYERS:
                kv = rmsnorm(h, kv_norm) @ w_kv
                pad = ((0, 0), (LEFT_CHUNKS * CHUNK, 0), (0, 0), (0, 0))
                k_pad = jnp.pad(kv[..., :B_WIDTH].reshape(bsz, seq, B_HEADS, B_HEAD_DIM), pad)
                v_pad = jnp.pad(kv[..., B_WIDTH:].reshape(bsz, seq, B_HEADS, B_HEAD_DIM), pad)
            j = layer - N_A_LAYERS
            h = h + chunk_attention(rmsnorm(h, b_norm[j]), b_w_q[j], b_rel_bias[j], b_w_out[j], k_pad, v_pad)
        h = h + conv_ffn(rmsnorm(h, f_norm[layer]), f_w_up[layer], f_conv[layer], f_conv_b[layer], f_w_down[layer])
    return rmsnorm(h, final_norm)


DEPTH_2 = 1

N_HEADS_SB = 8
HEAD_DIM_SB = 64
D_SB = N_HEADS_SB * HEAD_DIM_SB
N_GROUPS_SGU = 8
GROUP_DIM_SGU = 64
D_SGU = N_GROUPS_SGU * GROUP_DIM_SGU
SGU_CHUNK = 128
Q_BLOCK = 128
IN_WIDTHS = (D_SB, D_SB, D_SB, D_SB, D_SGU, D_SGU, D_SGU, D_MODEL, D_MODEL)
D_IN = 4 * D_SB + 3 * D_SGU + 2 * D_MODEL


def rmsnorm_2(x, g):
    xf = x.astype(jnp.float32)
    y = xf * lax.rsqrt(jnp.mean(xf * xf, axis=-1, keepdims=True) + EPS)
    return (y * g.astype(jnp.float32)).astype(x.dtype)

def split_points():
    pts, acc = [], 0
    for w in IN_WIDTHS[:-1]:
        acc += w
        pts.append(acc)
    return pts

def stick_breaking_attention(q, k, v):
    b, s, h, dh = q.shape
    scale = dh ** -0.5
    qf = q.astype(jnp.float32).transpose(0, 2, 1, 3) * scale
    kf = k.astype(jnp.float32).transpose(0, 2, 1, 3)
    vf = v.astype(jnp.float32).transpose(0, 2, 1, 3)
    outs = []
    for start in range(0, s, Q_BLOCK):
        end = start + Q_BLOCK
        qb = qf[:, :, start:end]
        kb = kf[:, :, :end]
        vb = vf[:, :, :end]
        z = jnp.einsum('bhqd,bhkd->bhqk', qb, kb)
        t_idx = start + jnp.arange(Q_BLOCK)[:, None]
        s_idx = jnp.arange(end)[None, :]
        before = s_idx < t_idx
        log_keep = jnp.where(before, jax.nn.log_sigmoid(-z), 0.0)
        log_stick = lax.cumsum(log_keep, axis=3, reverse=True) - log_keep
        log_w = jax.nn.log_sigmoid(z) + log_stick
        w = jnp.where(before, jnp.exp(log_w), 0.0)
        outs.append(jnp.einsum('bhqk,bhkd->bhqd', w, vb))
    o = jnp.concatenate(outs, axis=2)
    return o.transpose(0, 2, 1, 3).astype(q.dtype)

def spatial_gating(u, v, ln_g, ln_b, w_s, b_s):
    b, s, g, c = v.shape
    vf = v.astype(jnp.float32)
    mu = jnp.mean(vf, axis=-1, keepdims=True)
    var = jnp.mean(jnp.square(vf - mu), axis=-1, keepdims=True)
    vn = (vf - mu) * lax.rsqrt(var + EPS) * ln_g.astype(jnp.float32) + ln_b.astype(jnp.float32)
    vn = vn.reshape(b, s // SGU_CHUNK, SGU_CHUNK, g, c)
    pos = jnp.arange(SGU_CHUNK)
    mask = (pos[None, :] // CHUNK) <= (pos[:, None] // CHUNK)
    w = jnp.where(mask[None], w_s.astype(jnp.float32), 0.0)
    mixed = jnp.einsum('gts,bnsgc->bntgc', w, vn) + b_s.astype(jnp.float32).T[None, None, :, :, None]
    return u * mixed.reshape(b, s, g, c).astype(u.dtype)

def second_inputs(seed: int = 0) -> dict:
    key = jax.random.key(seed)
    ks = jax.random.split(key, 13)
    f32 = jnp.float32
    x = jax.random.normal(ks[0], (BATCH, SEQ, D_MODEL), f32)
    norm_g = 1.0 + 0.1 * jax.random.normal(ks[1], (DEPTH_2, D_MODEL), f32)
    w_in = jax.random.normal(ks[2], (DEPTH_2, D_MODEL, D_IN), f32) * D_MODEL ** -0.5
    sgu_ln_g = 1.0 + 0.1 * jax.random.normal(ks[3], (DEPTH_2, N_GROUPS_SGU, GROUP_DIM_SGU), f32)
    sgu_ln_b = 0.1 * jax.random.normal(ks[4], (DEPTH_2, N_GROUPS_SGU, GROUP_DIM_SGU), f32)
    w_spatial = jax.random.normal(ks[5], (DEPTH_2, N_GROUPS_SGU, SGU_CHUNK, SGU_CHUNK), f32) * SGU_CHUNK ** -0.5
    b_spatial = 1.0 + 0.1 * jax.random.normal(ks[6], (DEPTH_2, N_GROUPS_SGU, SGU_CHUNK), f32)
    w_up_a = jax.random.normal(ks[7], (DEPTH_2, D_SB, D_MODEL), f32) * D_SB ** -0.5
    w_up_b = jax.random.normal(ks[8], (DEPTH_2, D_SGU, D_MODEL), f32) * D_SGU ** -0.5
    w_out = jax.random.normal(ks[9], (DEPTH_2, D_MODEL, D_MODEL), f32) * D_MODEL ** -0.5
    final_norm_g = 1.0 + 0.1 * jax.random.normal(ks[10], (D_MODEL,), f32)
    return {'x': x, 'norm_g': norm_g, 'w_in': w_in, 'sgu_ln_g': sgu_ln_g, 'sgu_ln_b': sgu_ln_b,
            'w_spatial': w_spatial, 'b_spatial': b_spatial, 'w_up_a': w_up_a, 'w_up_b': w_up_b,
            'w_out': w_out, 'final_norm_g': final_norm_g}

def second_block(x, norm_g, w_in, sgu_ln_g, sgu_ln_b, w_spatial, b_spatial, w_up_a, w_up_b, w_out, final_norm_g):
    b, s, _ = x.shape
    pts = split_points()
    for l in range(DEPTH_2):
        h = rmsnorm_2(x, norm_g[l])
        proj = jnp.einsum('bsd,de->bse', h, w_in[l])
        q, k, v, z_a, u_b, v_b, z_b, g_a, g_b = jnp.split(proj, pts, axis=-1)
        y_a = stick_breaking_attention(
            q.reshape(b, s, N_HEADS_SB, HEAD_DIM_SB),
            k.reshape(b, s, N_HEADS_SB, HEAD_DIM_SB),
            v.reshape(b, s, N_HEADS_SB, HEAD_DIM_SB)).reshape(b, s, D_SB) * jax.nn.silu(z_a)
        y_b = spatial_gating(
            jax.nn.gelu(u_b).reshape(b, s, N_GROUPS_SGU, GROUP_DIM_SGU),
            jax.nn.gelu(v_b).reshape(b, s, N_GROUPS_SGU, GROUP_DIM_SGU),
            sgu_ln_g[l], sgu_ln_b[l], w_spatial[l], b_spatial[l]).reshape(b, s, D_SGU) * jax.nn.silu(z_b)
        p_a = jnp.einsum('bse,ed->bsd', y_a, w_up_a[l])
        p_b = jnp.einsum('bse,ed->bsd', y_b, w_up_b[l])
        merged = jax.nn.sigmoid(g_a) * p_a + jax.nn.sigmoid(g_b) * p_b
        x = x + jnp.einsum('bsd,de->bse', merged, w_out[l])
    return rmsnorm_2(x, final_norm_g)


def setup_inputs(seed=0):
    out = dict(first_inputs(seed))
    for name, value in second_inputs(seed + 1).items():
        if name != "x":
            out[name + "_2"] = value
    return out


def reference(
    x, a_norm, a_w_in, a_conv, a_A_log, a_dt_bias, a_out_norm, a_w_out, kv_norm, w_kv, b_norm,
    b_w_q, b_rel_bias, b_w_out, f_norm, f_w_up, f_conv, f_conv_b, f_w_down, final_norm,
    norm_g_2, w_in_2, sgu_ln_g_2, sgu_ln_b_2, w_spatial_2, b_spatial_2, w_up_a_2, w_up_b_2,
    w_out_2, final_norm_g_2,
):
    x = first_block(
        x, a_norm, a_w_in, a_conv, a_A_log, a_dt_bias, a_out_norm, a_w_out, kv_norm, w_kv,
        b_norm, b_w_q, b_rel_bias, b_w_out, f_norm, f_w_up, f_conv, f_conv_b, f_w_down,
        final_norm,
    )
    return second_block(
        x, norm_g_2, w_in_2, sgu_ln_g_2, sgu_ln_b_2, w_spatial_2, b_spatial_2, w_up_a_2,
        w_up_b_2, w_out_2, final_norm_g_2,
    )


_drawn_inputs = setup_inputs


def setup_inputs(seed=0):
    import zlib

    import numpy as np

    out = dict(_drawn_inputs(seed))
    spreads = {}
    factors = {'a_out_norm': 4.032,
     'kv_norm': 8.0,
     'b_norm': 8.0,
     'b_rel_bias': 5.647,
     'f_norm': 2.693,
     'f_conv_b': 5.509,
     'sgu_ln_g_2': 3.434,
     'sgu_ln_b_2': 3.077,
     'b_spatial_2': 2.938}
    for name, (base, spread) in spreads.items():
        noise = np.random.default_rng([zlib.crc32(name.encode()), seed]).standard_normal(out[name].shape)
        drawn = base * np.exp(spread * noise) if base else spread * noise
        out[name] = __import__('jax').numpy.asarray(drawn.astype(out[name].dtype))
    for name, factor in factors.items():
        out[name] = (out[name] * factor).astype(out[name].dtype)
    return out
```

```python
from contextlib import ExitStack

import concourse.bass as bass
from concourse import mybir

F32 = mybir.dt.float32
F32R = mybir.dt.float32r
ALU = mybir.AluOpType
ACT = mybir.ActivationFunctionType
AX_X = mybir.AxisListType.X

P = 128
S = 512
D = 1024
KD = D // P
NC = S // P
HA = 8
F = 2816
KF = F // P
KH = KF // 2
PAIRS = 8
SBP = 4
GPP = 4
EPS = 1e-6
NEG = -1e30
EXT = S - 1 + P
TRI = 10 * P
SEG = [6 * P, 3 * P, P, 0]
LEVELS = [2, 4, 8, 16, 32, 64]

C_ID, C_ONE, C_CUM, C_SUF, C_M1, C_INCL2, C_NEGD, C_LEV = 0, 1, 2, 3, 4, 5, 7, 8
NCONST = C_LEV + len(LEVELS)

G_A, G_KV, G_B, G_F, G_FIN, G_2, G_FIN2 = 0, 8, 16, 24, 40, 48, 56
V_ACONV = 64
V_FCONV = V_ACONV + 96
V_FBIAS = V_FCONV + 264
V_AOUT = V_FBIAS + 88
NVEC = V_AOUT + 1


class Stage:

    def __init__(self, n, bodies, kc, slots, first, landed, src):
        self.n, self.bodies, self.kc, self.slots = n, bodies, kc, slots
        self.first, self.landed, self.src = first, landed, src
        self.follow = None

    def number(self, i, j):
        return i * self.n + (self.first + j)


def plan():
    stages = {}
    first, landed, src = 3, [0, 1, 1, 1], [3, 0]
    stages["delta"] = Stage(4, 8, 8, 2, first, landed, 3)
    first, landed, src = 32, [8, 8, 8, 8], [32, 0]
    for name, n, bodies, kc, slots in (
            ("a_out", 4, 2, 8, 2), ("up0", 4, 11, 8, 2), ("down0", 4, 4, KH, 2),
            ("attn", 3, 8, 8, 3), ("b_out", 4, 2, 8, 2), ("up1", 4, 11, 8, 2), ("down1", 4, 4, KH, 2),
            ("stick_z", 4, 1, 8, 2), ("stick", 3, 4, 8, 3), ("sgu", 3, 4, 8, 3), ("merge", 3, 8, 8, 3), ("out", 4, 2, 8, 2)):
        which = 0 if kc == 8 else 1
        stages[name] = Stage(n, bodies, kc, slots, first, list(landed), src[which])
        first += n * bodies
        src[which] += n * bodies
        landed = [c + (bodies if j < n else 0) for j, c in enumerate(landed)]
    stages["n8"], stages["n11"] = src
    return stages


ORDER = ["delta", "a_out", "up0", "down0", "attn", "b_out", "up1", "down1", "stick_z", "stick", "sgu", "merge", "out"]


def build(nc, xT, w8, w11, w_gates, consts, vecs, a_log, dt_bias, rel_flip, ln_gb, w_spat, b_spat, outT,
          last_stage="out"):
    st = plan()
    stages = ORDER[:ORDER.index(last_stage) + 1]
    ctx = ExitStack()
    with ctx:
        top = [16512]
        LIMIT = 229344

        def sb(name, shape, dt=F32, at=None):
            size = 4
            for d in shape[1:]:
                size *= d
            size = (size + 31) // 32 * 32
            where = top[0] if at is None else at
            assert where + size <= LIMIT, (name, where + size - LIMIT)
            if at is None:
                top[0] = where + size
            return nc.alloc_sbuf_tensor_at(name, list(shape), dt, offset=where)

        class Region:

            def __init__(self, start):
                self.at = start

            def sb(self, name, shape, dt=F32):
                size = 4
                for d in shape[1:]:
                    size *= d
                t = sb(name, shape, dt, at=self.at)
                self.at += (size + 31) // 32 * 32
                return t

        made = {}

        def ev(name):
            if name not in made:
                made[name] = ctx.enter_context(nc.semaphore(name))
            return made[name]

        h = sb("h", [P, KD, S])
        wraw = sb("wraw", [P, 4 * KH * P])
        wsplit = sb("wsplit", [P, 6 * KD * P], F32R)
        cst = sb("cst", [P, NCONST, P])
        vec = sb("vec", [P, NVEC])
        ssq = sb("ssq", [P, S])
        rstd = sb("rstd", [P, S])
        epst = sb("epst", [P, 1])
        tmp = sb("tmp", [P, 2, S])
        tmp_more = sb("tmp_more", [P, 2, S], at=LIMIT - 4 * S * 4)
        xhi = sb("xhi", [P, KD, S], F32R)
        xlo = sb("xlo", [P, KD, S], F32R)
        scratch = top[0]

        r = Region(scratch)
        hid_hi = r.sb("hid_hi", [P, KF, S], F32R)
        hid_lo = r.sb("hid_lo", [P, KF, S], F32R)
        fy = r.sb("fy", [P, 4, S])

        r = Region(scratch)
        o_hi = r.sb("o_hi", [P, HA, S], F32R)
        o_lo = r.sb("o_lo", [P, HA, S], F32R)
        ys = r.sb("ys", [P, 4, S])
        sq = r.sb("sq", [P, 2, S])
        rqk = r.sb("rqk", [P, 2, S])
        kq = r.sb("kq", [P, NC, 2, P])
        kn = r.sb("kn", [P, S])
        qe = r.sb("qe", [P, S])
        crow = r.sb("crow", [P, S])
        brow = r.sb("brow", [P, S])
        ecrow = r.sb("ecrow", [P, S])
        dec = r.sb("dec", [P, NC, P])
        gd = r.sb("gd", [P, NC, 2, P])
        tn = r.sb("tn", [P, NC, P])
        tt = r.sb("tt", [P, NC, P])
        xm = r.sb("xm", [P, NC, P])
        kend = r.sb("kend", [P, NC, P])
        bv = r.sb("bv", [P, NC, P])
        rr = r.sb("rr", [P, NC, P])
        vn = r.sb("vn", [P, NC, P])
        state = r.sb("state", [P, P])
        wg = r.sb("wg", [P, KD, 16])
        wg_hi = r.sb("wg_hi", [P, KD, 16], F32R)
        wg_lo = r.sb("wg_lo", [P, KD, 16], F32R)
        alog = r.sb("alog", [P, HA])
        dtb = r.sb("dtb", [P, HA])
        beta = r.sb("beta", [P, HA, NC])
        gg = r.sb("gg", [P, HA, NC])
        cc = r.sb("cc", [P, HA, NC])
        kes = r.sb("kes", [P, HA, NC])
        ecl = r.sb("ecl", [P, HA, NC])
        nbe = r.sb("nbe", [P, HA, NC])
        t0 = r.sb("t0", [P, HA, NC])
        t1 = r.sb("t1", [P, HA, NC])
        rows = r.sb("rows", [HA * NC, 2, P])
        outputs = r.at
        osb = r.sb("osb", [P, S])
        sq_o = r.sb("sq_o", [P, S])
        ro = r.sb("ro", [P, S])
        oy = r.sb("oy", [P, S])
        assert outputs <= LIMIT - 4 * S * 4 <= r.at - 2 * S * 4

        r = Region(scratch + HA * S * 4)
        ext = r.sb("ext", [2 * PAIRS, EXT])
        relf = r.sb("relf", [2 * PAIRS, 513])
        negs = r.sb("negs", [64, 64])

        r = Region(scratch)
        xq_hi = r.sb("xq_hi", [P, KD, S], F32R)
        xq_lo = r.sb("xq_lo", [P, KD, S], F32R)
        ob_hi = r.sb("ob_hi", [P, PAIRS, S], F32R)
        ob_lo = r.sb("ob_lo", [P, PAIRS, S], F32R)
        at_k = r.sb("at_k", [P, S])
        at_q = r.sb("at_q", [P, S])
        at_v = r.sb("at_v", [P, S])
        at_vt = r.sb("at_vt", [P, NC, P])
        bias = r.sb("bias", [P, 2, S])
        prob = r.sb("prob", [P, 4, S])
        probT = r.sb("probT", [P, 2, S])
        nmax = r.sb("nmax", [P, 8])
        psum_ = r.sb("psum_", [P, 8])
        at_o = r.sb("at_o", [P, S])

        r = Region(scratch)
        ya_hi = r.sb("ya_hi", [P, SBP, S], F32R)
        ya_lo = r.sb("ya_lo", [P, SBP, S], F32R)
        yb_hi = r.sb("yb_hi", [P, GPP, S], F32R)
        yb_lo = r.sb("yb_lo", [P, GPP, S], F32R)
        second = r.at
        mg_hi = r.sb("mg_hi", [P, KD, S], F32R)
        mg_lo = r.sb("mg_lo", [P, KD, S], F32R)
        ga = r.sb("ga", [P, 2, S])
        mg = r.sb("mg", [P, 2, S])
        r = Region(second)
        sk_k = r.sb("sk_k", [P, S])
        sk_q = r.sb("sk_q", [P, S])
        sk_v = r.sb("sk_v", [P, S])
        sk_vt = r.sb("sk_vt", [P, NC, P])
        sk_z = r.sb("sk_z", [P, SBP, S])
        zs = r.sb("zs", [P, 2, TRI])
        sp = r.sb("sp", [P, 2, TRI])
        sw = r.sb("sw", [P, 2, TRI])
        sk_o = r.sb("sk_o", [P, S])
        r = Region(second)
        gu = r.sb("gu", [P, S])
        gv = r.sb("gv", [P, S])
        gz = r.sb("gz", [P, S])
        xc = r.sb("xc", [P, NC * 2, 64])
        xs2 = r.sb("xs2", [P, NC * 2, 64])
        mu = r.sb("mu", [P, NC * 2])
        var = r.sb("var", [P, NC * 2])
        gy = r.sb("gy", [P, S])
        wsp = r.sb("wsp", [P, 2 * GPP, P])
        wcur = r.sb("wcur", [P, 2, P])
        bsp = r.sb("bsp", [P, GPP, P])
        lngb = r.sb("lngb", [P, 2, GPP, P])

        acc = ctx.enter_context(nc.psum_tensor("acc", [P, 3, S], F32))
        pa = ctx.enter_context(nc.psum_tensor("pa", [P, 2, S], F32))
        pb = ctx.enter_context(nc.psum_tensor("pb", [P, S], F32))
        pc = ctx.enter_context(nc.psum_tensor("pc", [P, S], F32))
        pd = ctx.enter_context(nc.psum_tensor("pd", [P, S], F32))

        ext_dram = nc.dram_tensor("ext_dram", [2 * PAIRS, EXT], F32, kind="Internal").ap()
        bias_dram = nc.dram_tensor("bias_dram", [2 * PAIRS, P, S], F32, kind="Internal").ap()
        row_dram = nc.dram_tensor("row_dram", [2, HA * NC, P], F32, kind="Internal").ap()

        eps_d = epst[:, 0:1]
        ident = cst[:, C_ID, :]
        ones = cst[:, C_ONE, :]

        raw_landed = [ev(f"raw_landed{j}") for j in range(4)]
        w_hi_ready, w_lo_ready = ev("w_hi_ready"), ev("w_lo_ready")
        acc_done, acc_free = ev("acc_done"), ev("acc_free")

        def raw(s, j):
            return wraw[:, j * KH * P:(j * KH + s.kc) * P]

        def split(s, j, part):
            room = 2 * KH if s.slots == 2 else 2 * KD
            at = (j % s.slots) * room + part * s.kc
            return wsplit[:, at * P:(at + s.kc) * P]

        for name, after in zip(stages, stages[1:]):
            if st[name].slots == st[after].slots:
                st[name].follow = st[after]

        def normed(k):
            return tmp[:, k % 4, :] if k % 4 < 2 else tmp_more[:, k % 4 - 2, :]

        def chunks(ap):
            return ap.rearrange("p (t q) -> p t q", t=NC)

        def over_chunks(ap):
            return ap.unsqueeze(1).to_broadcast([P, NC, P])

        def each(eng, count, body):
            if count > 1:
                with eng.Fori(0, count - 1) as i:
                    body(i, False)
            body(count - 1, True)

        def each_ahead(eng, count, body):
            with eng.Fori(0, count - 2) as i:
                body(i, 2)
            body(count - 2, 1)
            body(count - 1, 0)

        block = ctx.enter_context(nc.Block())

        @block.sync
        def _(sp):
            for n in range(2):
                half = slice(n * KD // 2, (n + 1) * KD // 2)
                sp.dma_start(h[:, half, :], xT[:, half, :]).then_inc(ev(f"x_landed{n}"), 16)
            sp.dma_start(cst[:], consts).then_inc(ev("consts_landed"), 16)
            sp.dma_start(vec[:], vecs).then_inc(ev("consts_landed"), 16)
            sp.dma_start(wg[:], w_gates).then_inc(ev("gates_landed"), 16)
            sp.dma_start(alog[:], a_log.partition_broadcast(P)).then_inc(ev("gates_landed"), 16)
            sp.dma_start(dtb[:], dt_bias.partition_broadcast(P)).then_inc(ev("gates_landed"), 16)

            def load(s, i, j):
                dram = w8 if s.kc == KD else w11
                sp.dma_start(raw(s, j), dram[i * s.n + (s.src + j), :, :]).then_inc(raw_landed[j], 16)

            for name in stages:
                s = st[name]
                if name == "delta":
                    for j in (1, 2, 3):
                        load(s, -1, j)
                    load(s, 0, 0)
                    for j in (1, 2, 3):
                        sp.wait_ge(w_lo_ready, j)
                        load(s, 0, j)
                    with sp.Fori(1, s.bodies - 1) as i:
                        for j in range(4):
                            sp.wait_ge(w_lo_ready, i * 4 + j)
                            load(s, i, j)
                    sp.wait_ge(w_lo_ready, s.number(s.bodies - 1, 0) - 3)
                    load(s, s.bodies - 1, 0)
                    continue
                sp.wait_ge(w_lo_ready, s.first)
                for j in range(s.n):
                    load(s, 0, j)
                if s.bodies > 1:
                    with sp.Fori(1, s.bodies) as i:
                        for j in range(s.n):
                            sp.wait_ge(w_lo_ready, s.number(i, j) + 1 - s.n)
                            load(s, i, j)
            sp.wait_ge(ev("final_ready"), KD)
            sp.dma_start(outT, h[:]).then_inc(ev("stored"), 16)
            sp.wait_ge(ev("stored"), 16)

        @block.gpsimd
        def _(pool):
            pool.dma_start(relf[:], rel_flip).then_inc(ev("rel_landed"), 16)
            nc.gpsimd.memset(negs[:], NEG).then_inc(ev("negs_ready"), 1)
            pool.wait_ge(ev("ext_ready"), 2)
            pool.dma_start(ext_dram, ext[:]).then_inc(ev("bias_table"), 16)
            pool.wait_ge(ev("bias_table"), 16)
            pool.dma_start(bias_dram, bass.AP(ext_dram.tensor, P - 1, [[EXT, 2 * PAIRS], [-1, P], [1, S]])
                           ).then_inc(ev("bias_table"), 16)
            pool.wait_ge(ev("bias_table"), 32)
            pool.wait_ge(ev("negs_ready"), 1)
            pool.dma_start(bias_dram[:, 0:64, S - 64:S].rearrange("h p x -> p h x"),
                           negs[:].unsqueeze(1).to_broadcast([64, 2 * PAIRS, 64])).then_inc(ev("bias_table"), 16)

            pool.wait_ge(ev("rows_ready"), 1)
            pool.dma_start(row_dram.rearrange("a r p -> r a p"), rows[:]).then_inc(ev("rows_stored"), 16)
            pool.wait_ge(ev("rows_stored"), 16)
            row_src = row_dram.rearrange("a (h r) p -> a h (r p)", h=HA)

            def load_rows(i):
                pool.dma_start(crow[:], row_src[0, i, :].partition_broadcast(P)).then_inc(ev("crow_landed"), 16)
                pool.dma_start(brow[:], row_src[1, i, :].partition_broadcast(P)).then_inc(ev("brow_landed"), 16)

            load_rows(0)
            with pool.Fori(1, HA) as i:
                pool.wait_ge(ev("ecrow_ready"), i)
                pool.wait_ge(ev("dec_exponent"), i)
                load_rows(i)

            if "attn" in stages:
                pool.wait_ge(ev("bias_table"), 48)
                pool.wait_ge(acc_free, st["attn"].first)

                def load_bias(i):
                    pool.dma_start(bias[:], bias_dram.rearrange("(i e) p x -> i p e x", e=2)[i, :, :, :]
                                   ).then_inc(ev("bias_landed"), 16)
                load_bias(0)
                with pool.Fori(1, PAIRS) as i:
                    pool.wait_ge(ev("biased"), i * 8)
                    load_bias(i)
            if "sgu" in stages:
                pool.wait_ge(ev("ya_lo_ready"), SBP)
                pool.wait_ge(acc_free, st["sgu"].first)
                pool.dma_start(wsp[:], w_spat).then_inc(ev("wsp_landed"), 16)
                for e in range(2):
                    src = b_spat.rearrange("(i e) t -> e i t", e=2)[e]
                    pool.dma_start(bsp[64 * e:64 * e + 64], src.partition_broadcast(64)).then_inc(ev("bsp_landed"), 16)
                pool.dma_start(lngb[:], ln_gb.partition_broadcast(P)).then_inc(ev("lngb_landed"), 16)
                pool.wait_ge(ev("wsp_landed"), 16)
                nc.gpsimd.memset(wsp[64:P, :, 0:64], 0.0).then_inc(ev("wsp_ready"), 1)
                pool.wait_ge(ev("wsp_ready"), 1)
                with pool.Fori(0, GPP) as i:
                    pool.wait_ge(ev("mixed"), i)
                    nc.gpsimd.tensor_copy(wcur[:], wsp[:].rearrange("p (i e) t -> p i e t", e=2)[:, i, :, :]
                                          ).then_inc(ev("wcur_ready"), 1)

        @block.tensor
        def _(pe):
            mm = nc.tensor.matmul
            turn = nc.tensor.transpose

            def product(s, j, out, a, b, k0, k1, x_at=0, first=0, last=None):
                last = s.kc - 1 if last is None else last
                whi = split(s, j, 0).rearrange("p (k n) -> p k n", k=s.kc)
                wlo = split(s, j, 1).rearrange("p (k n) -> p k n", k=s.kc)
                for k in range(k0, k1):
                    mm(out, whi[:, k, :], a[:, x_at + k, :], start=(k == first), stop=False)
                    mm(out, whi[:, k, :], b[:, x_at + k, :], start=False, stop=False)
                    m = mm(out, wlo[:, k, :], a[:, x_at + k, :], start=False, stop=(k == last))
                return m

            def tile(s, i, j, a=xhi, b=xlo, k0=0, k1=KD):
                if k0 == 0:
                    pe.wait_ge(w_lo_ready, s.number(i, j) + 1)
                    if s.first >= 32 or not isinstance(i, int) or s.number(i, j) >= s.slots:
                        pe.wait_ge(acc_free, s.number(i, j) + 1 - s.slots)
                m = product(s, j, acc[:, j % s.slots, :], a, b, k0, k1)
                if k1 == KD:
                    m.then_inc(acc_done, 1)

            def norm(n):
                pe.wait_ge(ev("ssq_added"), KD * (n + 1))
                mm(pd[:], ones, ssq[:], start=True, stop=True).then_inc(ev("norm_sum"), 1)

            def opening(s, m, i=0, js=(0, 1), a=xhi, b=xlo):
                for k in range(KD):
                    pe.wait_ge(ev("x_lo_ready"), KD * m + k + 1)
                    for j in js:
                        tile(s, i, j, a, b, k0=k, k1=k + 1)

            pe.wait_ge(ev("consts_landed"), 32)
            norm(0)
            s = st["delta"]
            opening(s, 0, -1, (1, 2))

            pe.wait_ge(ev("wg_lo_ready"), 1)
            for k in range(KD):
                mm(acc[0:16, 2, :], wg_hi[:, k, :], xhi[:, k, :], start=(k == 0), stop=False)
                mm(acc[0:16, 2, :], wg_hi[:, k, :], xlo[:, k, :], start=False, stop=False)
                m = mm(acc[0:16, 2, :], wg_lo[:, k, :], xhi[:, k, :], start=False, stop=(k == KD - 1))
            m.then_inc(ev("gates_done"), 1)
            pe.wait_ge(ev("gates_copied"), 1)
            for t in range(NC):
                m = turn(pb[:, t * 16:(t + 1) * 16], sq[0:16, 0, t * P:t * P + P], cst[0:16, C_ID, 0:16])
            m.then_inc(ev("gates_turned"), 1)

            tile(s, -1, 3)

            pe.wait_ge(ev("gg_ready"), 1)
            gcols = gg[:].rearrange("p h t -> p (h t)")
            mm(pb[:, 0:32], cst[:, C_CUM, :], gcols, start=True, stop=True)
            mm(pb[:, 32:64], ones, gcols, start=True, stop=True).then_inc(ev("cum_done"), 1)
            pe.wait_ge(ev("cc_ready"), 1)
            turn(pc[0:32, 0:P], cc[:].rearrange("p h t -> p (h t)"), ident)
            turn(pc[0:32, P:2 * P], beta[:].rearrange("p h t -> p (h t)"), ident).then_inc(ev("rows_turned"), 1)
            pe.wait_ge(ev("rows_ready"), 1)
            pe.wait_ge(ev("kes_diff"), 1)
            pe.wait_ge(ev("ecl_ready"), 1)

            NL = len(LEVELS)

            def qk_norms(i):
                pe.wait_ge(ev("qk_squared"), i + 1)
                mm(pa[:, 0, :], ones, sq[:, 0, :], start=True, stop=True)
                mm(pa[:, 1, :], ones, sq[:, 1, :], start=True, stop=True).then_inc(ev("qk_sums"), 1)

            def out_pieces(done, upto):
                if done == 0:
                    pe.wait_ge(acc_free, st["a_out"].first)
                    pe.wait_ge(ev("o_lo_ready"), HA - 1)
                for c in range(done, upto):
                    j, k = c // (HA - 1), c % (HA - 1)
                    tile(st["a_out"], 0, j, o_hi, o_lo, k0=k, k1=k + 1)

            def delta(i, last):
                tile(s, i, 0)
                pe.wait_ge(ev("kn_ready"), i + 1)
                for t in range(NC):
                    m = turn(pb[:, t * P:t * P + P], kn[:, t * P:t * P + P], ident)
                m.then_inc(ev("k_turned"), 1)
                for t in range(NC):
                    m = turn(pc[:, t * P:t * P + P], ys[:, 2, t * P:t * P + P], ident)
                m.then_inc(ev("v_turned"), 1)
                pe.wait_ge(ev("kb_ready"), i + 1)
                for t in range(NC):
                    m = mm(pa[:, t // 2, (t % 2) * 2 * P:(t % 2 + 1) * 2 * P], kn[:, t * P:t * P + P],
                           kq[:, t, :, :].rearrange("p a q -> p (a q)"), start=True, stop=True)
                m.then_inc(ev("gram_done"), 1)
                if not last:
                    tile(s, i, 1)
                pe.wait_ge(ev("tt_ready"), i * (NL + 1) + 1)
                pe.wait_ge(ev("o_ln"), i)
                for t in range(NC):
                    m = turn(pd[:, t * P:t * P + P], tt[:, t, :], ident)
                m.then_inc(ev("tn_turned"), 1)
                pe.wait_ge(ev("kend_ready"), i + 1)
                pe.wait_ge(ev("bv_ready"), i + 1)
                for n in range(NL):
                    pe.wait_ge(ev("tn_ready"), i * NL + (n + 1))
                    for t in range(NC):
                        m = mm(pb[:, t * P:t * P + P], gd[:, t, 0, :], tn[:, t, :], start=True, stop=True)
                    m.then_inc(ev("x_done"), 1)
                    if last:
                        out_pieces(2 * n, 2 * n + 2)
                    if not last:
                        tile(s, i, 2 + n // 3, k0=[0, 3, 6, 1, 4, 6][n], k1=[2, 5, 8, 3, 6, 8][n])
                    pe.wait_ge(ev("xm_ready"), i * NL + (n + 1))
                    pe.wait_ge(ev("tt_ready"), i * (NL + 1) + (n + 1))
                    if n < NL - 1:
                        for t in range(NC):
                            m = mm(pc[:, t * P:t * P + P], tt[:, t, :], xm[:, t, :], start=True, stop=True)
                        m.then_inc(ev("join_done"), 1)
                    for t in range(NC):
                        m = mm(pd[:, t * P:t * P + P], xm[:, t, :], tt[:, t, :], start=True, stop=True)
                    m.then_inc(ev("join_done"), 1)
                    if not last and n in (0, 1, 2, 3):
                        tile(s, i, 2 + (n + 1) // 3, k0=[2, 5, 0, 3][n], k1=[3, 6, 1, 4][n])
                pe.wait_ge(ev("tt_ready"), (i + 1) * (NL + 1))
                for t in range(NC):
                    q = slice(t * P, t * P + P)
                    if t > 0:
                        pe.wait_ge(ev("state_ready"), i * (NC - 1) + t)
                        mm(pb[:, q], kn[:, q], state[:], start=True, stop=True).then_inc(ev("ks_done"), 1)
                        mm(acc[:, 2, q], state[:], qe[:, q], start=True, stop=False)
                        pe.wait_ge(ev("r_ready"), i * (NC - 1) + t)
                        mm(pc[:, q], tt[:, t, :], rr[:, t, :], start=True, stop=True).then_inc(ev("v_done"), 1)
                    else:
                        mm(pc[:, q], tt[:, t, :], bv[:, t, :], start=True, stop=True).then_inc(ev("v_done"), 1)
                    pe.wait_ge(ev("vn_ready"), i * NC + (t + 1))
                    if t < NC - 1:
                        mm(pd[:, q], kend[:, t, :], vn[:, t, :], start=True, stop=True).then_inc(ev("s_done"), 1)
                    m = mm(acc[:, 2, q], vn[:, t, :], gd[:, t, 1, :], start=(t == 0), stop=True)
                m.then_inc(ev("o_done"), 1)
                if last:
                    out_pieces(12, 14)
                if not last:
                    qk_norms(i + 1)
                pe.wait_ge(ev("o_squared"), i + 1)
                mm(pd[:], ones, sq_o[:], start=True, stop=True).then_inc(ev("o_sums"), 1)

            qk_norms(0)
            each(pe, HA, delta)

            def residual(name, a, b):
                s = st[name]
                pe.wait_ge(acc_free, s.first)
                for j in range(s.n):
                    tile(s, 0, j, a, b, k0=KD - 1 if name == "a_out" and j < 2 else 0)
                with pe.Fori(1, s.bodies) as i:
                    for j in range(s.n):
                        tile(s, i, j, a, b)

            def ffn(layer, m):
                s = st[f"up{layer}"]
                pe.wait_ge(acc_free, s.first)
                opening(s, m)
                tile(s, 0, 2)
                tile(s, 0, 3)
                with pe.Fori(1, s.bodies) as i:
                    for j in range(s.n):
                        tile(s, i, j)
                s = st[f"down{layer}"]
                pe.wait_ge(acc_free, s.first - 1)
                with pe.Fori(0, s.bodies) as i:
                    for j in range(s.n):
                        pe.wait_ge(w_lo_ready, s.number(i, j) + 1)
                        if j < 2:
                            pe.wait_ge(ev("hid_lo_ready"), KF * layer + KH * (j + 1))
                        if j % 2 == 0:
                            pe.wait_ge(acc_free, s.number(i, j) - 2)
                        product(s, j, acc[:, j // 2, :], hid_hi, hid_lo, 0, KH, x_at=(j % 2) * KH,
                                first=0 if j % 2 == 0 else -1, last=KH - 1 if j % 2 else -1
                                ).then_inc(acc_done, 1)

            def pieces(s, i, done, upto, last_x=(xhi, xlo)):
                while done < upto:
                    j, k0 = done // KD, done % KD
                    k1 = min(KD, k0 + upto - done)
                    tile(s, i, j, *(last_x if j == 2 else (xhi, xlo)), k0=k0, k1=k1)
                    done += k1 - k0

            def attention():
                s = st["attn"]
                pe.wait_ge(acc_free, s.first)
                opening(s, 2)
                opening(s, 3, js=(2,), a=xq_hi, b=xq_lo)
                ahead = [0, 2, 4, 7, 9, 11, 14, 16, 19, 22, 24, 24]

                def body(i, more):
                    pe.wait_ge(acc_free, s.number(i, 1) + 1)
                    pe.wait_ge(ev("probT_ready"), i * 8)
                    for t in range(NC):
                        m = turn(pb[:, t * P:t * P + P], at_v[:, t * P:t * P + P], ident)
                    m.then_inc(ev("at_v_turned"), 1)
                    pe.wait_ge(acc_free, s.number(i, 2) + 1)
                    pe.wait_ge(ev("at_o_read"), i)
                    for step in range(8 + 3):
                        if step < 8:
                            u, e, b = step, step // 4, step % 4
                            c = slice(64 * e, 64 * e + 64)
                            pe.wait_ge(ev("biased"), i * 8 + u - 1 if u >= 2 else i * 8)
                            mm(pa[:, u % 2, 0:(b + 1) * P], at_q[c, b * P:b * P + P], at_k[c, 0:(b + 1) * P],
                               start=True, stop=True).then_inc(ev("scores_done"), 1)
                        if more:
                            pieces(s, i + 1, ahead[step], ahead[step + 1], (xq_hi, xq_lo))
                        if 2 <= step < 10:
                            u, b = step - 2, (step - 2) % 4
                            pe.wait_ge(ev("prob_ready"), i * 8 + (u + 1))
                            if u >= 2:
                                pe.wait_ge(ev("probT_ready"), i * 8 + (u - 1))
                            else:
                                pe.wait_ge(ev("at_vt_ready"), i + 1)
                            for k in range(b + 1):
                                m = turn([pb, pc][u % 2][:, k * P:k * P + P], prob[:, u % 4, k * P:k * P + P], ident)
                            m.then_inc(ev("prob_turned"), 1)
                        if step >= 3:
                            u, e, b = step - 3, (step - 3) // 4, (step - 3) % 4
                            pe.wait_ge(ev("probT_ready"), i * 8 + (u + 1))
                            for k in range(b + 1):
                                m = mm(pd[64 * e:64 * e + 64, b * P:b * P + P], at_vt[:, k, 64 * e:64 * e + 64],
                                       probT[:, u % 2, k * P:k * P + P], start=(k == 0), stop=(k == b))
                            m.then_inc(ev("pv_done"), 1)
                each_ahead(pe, PAIRS, body)

            def stick():
                s = st["stick"]
                pe.wait_ge(acc_free, s.first)
                pieces(s, 0, 0, 3 * KD)
                ahead = [0, 2, 5, 8, 11, 13, 16, 19, 22, 24, 24]

                def body(i, more):
                    pe.wait_ge(acc_free, s.number(i, 2) + 1)
                    for t in range(NC):
                        m = turn(pb[:, t * P:t * P + P], sk_v[:, t * P:t * P + P], ident)
                    m.then_inc(ev("sk_v_turned"), 1)
                    pe.wait_ge(ev("sk_o_ready"), i)
                    for step in range(8 + 2):
                        if step < 8:
                            u, e, k = step, step // 4, 3 - step % 4
                            c = slice(64 * e, 64 * e + 64)
                            if u >= 2:
                                pe.wait_ge(ev("zs_ready"), i * 8 + (u - 1))
                            mm(pa[:, u % 2, 0:(4 - k) * P], sk_k[c, k * P:k * P + P], sk_q[c, k * P:S],
                               start=True, stop=True).then_inc(ev("logits_done"), 1)
                        if more:
                            pieces(s, i + 1, ahead[step], ahead[step + 1])
                        if step >= 2:
                            u, e, k = step - 2, (step - 2) // 4, 3 - (step - 2) % 4
                            out = [pb, pc][u % 2]
                            pe.wait_ge(ev("sp_ready"), i * 8 + (u + 1))
                            if u >= 2:
                                pe.wait_ge(ev("drest"), i * 8 + (u - 1))
                            else:
                                pe.wait_ge(ev("sk_vt_ready"), i + 1)
                            for kk in range(k, NC):
                                lhs = cst[:, C_SUF, :] if kk == k else ones
                                m = mm(out[:, (kk - k) * P:(4 - k) * P], lhs, sp[:, e, SEG[kk]:SEG[kk] + (4 - kk) * P],
                                       start=(kk == k), stop=(kk == 3))
                            m.then_inc(ev("suffix_done"), 1)
                    for e in range(2):
                        pe.wait_ge(ev("sw_ready"), i * 8 + (4 * e + 4))
                        for k in range(NC):
                            m = mm(pd[64 * e:64 * e + 64, k * P:S], sk_vt[:, k, 64 * e:64 * e + 64],
                                   sw[:, e, SEG[k]:SEG[k] + (4 - k) * P], start=(k == 0), stop=(k == 3))
                    m.then_inc(ev("sk_o_done"), 1)
                each_ahead(pe, SBP, body)

            def gating():
                s = st["sgu"]
                pe.wait_ge(acc_free, s.first)
                pieces(s, 0, 0, 3 * KD)

                def body(i, last):
                    pe.wait_ge(acc_free, s.number(i, 0) + 1)
                    for t in range(NC):
                        m = turn(pb[:, t * P:t * P + P], gv[:, t * P:t * P + P], ident)
                    m.then_inc(ev("gv_turned"), 1)
                    if not last:
                        pieces(s, i + 1, 0, 3 * KD)
                    pe.wait_ge(ev("vn_spatial_ready"), i + 1)
                    pe.wait_ge(ev("wcur_ready"), i + 1)
                    pe.wait_ge(ev("mixed_read"), i)
                    for e in range(2):
                        for t in range(NC):
                            m = mm(pc[64 * e:64 * e + 64, t * P:t * P + P], xc[:, 2 * t + e, :], wcur[:, e, :],
                                   start=True, stop=True)
                    m.then_inc(ev("mixed"), 1)
                each(pe, GPP, body)

            def merge():
                s = st["merge"]
                pe.wait_ge(acc_free, s.first)
                with pe.Fori(0, s.bodies) as i:
                    tile(s, i, 0)
                    tile(s, i, 1)
                    pe.wait_ge(w_lo_ready, s.number(i, 2) + 1)
                    pe.wait_ge(acc_free, s.number(i, 2) - 2)
                    product(s, 2, acc[:, 2, :], ya_hi, ya_lo, 0, 4, last=3)
                    product(s, 2, pa[:, 0, :], yb_hi, yb_lo, 4, 8, x_at=-4, first=4).then_inc(acc_done, 1)

            n = 1

            if "a_out" in stages:
                pe.wait_ge(ev("o_lo_ready"), HA)
                residual("a_out", o_hi, o_lo)
            if "up0" in stages:
                norm(n)
                n += 1
                ffn(0, 1)
            if "attn" in stages:
                norm(n)
                n += 1
                attention()
            if "b_out" in stages:
                pe.wait_ge(ev("ob_lo_ready"), PAIRS)
                residual("b_out", ob_hi, ob_lo)
            if "up1" in stages:
                norm(n)
                n += 1
                ffn(1, 4)
            if "stick" in stages:
                norm(n)
                n += 1
                norm(n)
                n += 1
                s = st["stick_z"]
                pe.wait_ge(acc_free, s.first)
                opening(s, 5)
                tile(s, 0, 2)
                tile(s, 0, 3)
                stick()
            if "sgu" in stages:
                gating()
            if "merge" in stages:
                pe.wait_ge(ev("yb_lo_ready"), GPP)
                merge()
            if "out" in stages:
                pe.wait_ge(ev("mg_lo_ready"), KD)
                residual("out", mg_hi, mg_lo)
            norm(n)

        @block.scalar
        def _(act):
            A = nc.scalar.activation
            tables = nc.scalar.preload_act_table_set

            def cast(s, i, j):
                act.wait_ge(raw_landed[j], i * 16 + 16 * (s.landed[j] + 1))
                A(split(s, j, 0), raw(s, j), ACT.Copy).then_inc(w_hi_ready, 1)

            def cast_ahead(s, i, j, last):
                act.wait_ge(acc_done, s.number(i, j) + 1)
                if j + s.slots < s.n:
                    cast(s, i, j + s.slots)
                elif not last:
                    cast(s, i + 1, j + s.slots - s.n)
                elif s.follow:
                    cast(s.follow, 0, j + s.slots - s.n)

            def open_stage(name, js=None):
                s = st[name]
                act.wait_ge(acc_done, s.first)
                for j in js or range(s.slots):
                    cast(s, 0, j)

            def cast_x(m, hi):
                for k in range(KD):
                    act.wait_ge(ev("xn_ready"), KD * m + k + 1)
                    A(hi[:, k, :], normed(k), ACT.Copy).then_inc(ev("x_hi_ready"), 1)

            def root(n):
                act.wait_ge(ev("norm_sum"), n + 1)
                A(rstd[:], pd[:], ACT.Ln, bias=eps_d, scale=1.0 / D).then_inc(ev("norm_ln"), 1)
                act.wait_ge(ev("norm_ln"), n + 1)
                A(rstd[:], rstd[:], ACT.Exp, scale=-0.5).then_inc(ev("rstd_ready"), 1)

            tables("natural_log_exp_and_others")
            for k in range(KD):
                if k % (KD // 2) == 0:
                    act.wait_ge(ev(f"x_landed{k // (KD // 2)}"), 16)
                if k >= 4:
                    act.wait_ge(ev("ssq_added"), k - 3)
                A(normed(k), h[:, k, :], ACT.Square).then_inc(ev("h_squared"), 1)
            act.wait_ge(ev("gates_landed"), 48)
            A(wg_hi[:], wg[:], ACT.Copy).then_inc(ev("wg_hi_ready"), 1)
            s = st["delta"]
            cast(s, -1, 1)
            cast(s, -1, 2)
            act.wait_ge(ev("eps_ready"), 1)
            root(0)
            cast_x(0, xhi)

            act.wait_ge(ev("gates_landed"), 48)
            A(alog[:], alog[:], ACT.Exp).then_inc(ev("alog_exp"), 1)
            act.wait_ge(ev("gates_done"), 1)
            A(sq[0:16, 0, :], acc[0:16, 2, :], ACT.Copy).then_inc(ev("gates_copied"), 1)
            act.wait_ge(ev("gates_turned"), 1)
            gates = pb[:, 0:64].rearrange("p (t c) -> p c t", c=16)
            A(t0[:], gates[:, 0:8, :], ACT.Exp, scale=-1.0).then_inc(ev("beta_exp"), 1)
            act.wait_ge(ev("gate_abs"), 1)
            A(t1[:], t1[:], ACT.Exp, scale=-1.0).then_inc(ev("gate_exp"), 1)
            act.wait_ge(ev("gate_exp"), 1)
            A(t1[:], t1[:], ACT.Ln, bias=1.0).then_inc(ev("gate_ln"), 1)

            def conv_newest(j, head):
                w = vec[:, V_ACONV + 32 * (j - 1):V_ACONV + 32 * j].rearrange("p (h t) -> p h t", t=4)
                A(ys[:, j - 1, :], acc[:, j % 2, :], ACT.Copy, scale=w[:, head, 3:4]).then_inc(ev("conv_newest"), 1)

            def silu(i, j):
                act.wait_ge(acc_free, s.number(i, j) + 1)
                A(ys[:, j - 1, :], ys[:, j - 1, :], ACT.Silu).then_inc(ev("qkv_silu"), 1)

            def square_qk(i):
                act.wait_ge(ev("qkv_silu"), i * 3 + 5)
                A(sq[:, 0, :], ys[:, 0, :], ACT.Square)
                A(sq[:, 1, :], ys[:, 1, :], ACT.Square).then_inc(ev("qk_squared"), 1)

            act.wait_ge(ev("consts_landed"), 32)
            for j in (1, 2, 3):
                act.wait_ge(acc_done, j)
                if j == 1:
                    cast(s, -1, 3)
                else:
                    cast(s, 0, j - 2)
                conv_newest(j, 0)
            act.wait_ge(ev("kes_diff"), 1)
            A(ecl[:].rearrange("p h t -> p (h t)"), pb[:, 32:64], ACT.Exp).then_inc(ev("ecl_ready"), 1)
            A(nbe[:], cc[:], ACT.Exp).then_inc(ev("nbe_exp"), 1)
            A(kes[:], kes[:], ACT.Exp).then_inc(ev("kes_ready"), 1)
            tables("silu_and_others")
            silu(-1, 1)
            silu(-1, 2)
            square_qk(-1)
            silu(-1, 3)

            def qk_norms(i):
                act.wait_ge(ev("qk_sums"), i + 1)
                A(rqk[:], pa[:], ACT.Ln, bias=eps_d).then_inc(ev("rqk_ln"), 1)
                act.wait_ge(ev("rqk_ln"), i + 1)
                A(rqk[:], rqk[:], ACT.Exp, scale=-0.5).then_inc(ev("rqk_ready"), 1)

            def delta(i, last, last_qkv=False):
                act.wait_ge(ev("crow_landed"), i * 16 + 16)
                A(ecrow[:], crow[:], ACT.Exp).then_inc(ev("ecrow_ready"), 1)
                if last:
                    act.wait_ge(acc_done, s.number(i, 0) + 1)
                else:
                    cast_ahead(s, i, 0, False)
                A(ys[:, 3, :], acc[:, 0, :], ACT.Copy).then_inc(acc_free, 1)
                act.wait_ge(ev("dec_exponent"), i + 1)
                A(dec[:], dec[:], ACT.Exp).then_inc(ev("dec_ready"), 1)
                act.wait_ge(ev("k_turned"), i + 1)
                for t in range(NC):
                    x = A(kend[:, t, :], pb[:, t * P:t * P + P], ACT.Copy, scale=kes[:, i, t:t + 1])
                x.then_inc(ev("kend_ready"), 1)
                act.wait_ge(ev("v_turned"), i + 1)
                for t in range(NC):
                    x = A(bv[:, t, :], pc[:, t * P:t * P + P], ACT.Copy, scale=beta[:, i, t:t + 1])
                x.then_inc(ev("bv_ready"), 1)
                if not last:
                    cast_ahead(s, i, 1, False)
                    conv_newest(1, i + 1)
                    cast_ahead(s, i, 2, False)
                    conv_newest(2, i + 1)
                    tables("silu_and_others")
                    silu(i, 1)
                    act.wait_ge(acc_free, s.number(i, 0) + 1)
                    A(ys[:, 3, :], ys[:, 3, :], ACT.Silu).then_inc(ev("z_silu"), 1)
                    silu(i, 2)
                    square_qk(i)
                    act.wait_ge(acc_done, s.number(i, 3) + 1)
                    if not last_qkv:
                        cast(s, i + 1, 1)
                    conv_newest(3, i + 1)
                else:
                    open_stage("a_out")
                    tables("silu_and_others")
                    act.wait_ge(acc_free, s.number(i, 0) + 1)
                    A(ys[:, 3, :], ys[:, 3, :], ACT.Silu).then_inc(ev("z_silu"), 1)
                for t in range(NC):
                    act.wait_ge(ev("v_done"), i * NC + (t + 1))
                    A(vn[:, t, :], pc[:, t * P:t * P + P], ACT.Copy).then_inc(ev("vn_ready"), 1)
                if not last:
                    silu(i, 3)
                act.wait_ge(ev("o_done"), i + 1)
                A(osb[:], acc[:, 2, :], ACT.Copy)
                A(sq_o[:], acc[:, 2, :], ACT.Square).then_inc(ev("o_squared"), 1)
                tables("natural_log_exp_and_others")
                if not last:
                    qk_norms(i + 1)
                act.wait_ge(ev("o_sums"), i + 1)
                A(ro[:], pd[:], ACT.Ln, bias=eps_d, scale=1.0 / P).then_inc(ev("o_ln"), 1)
                act.wait_ge(ev("o_ln"), i + 1)
                A(ro[:], ro[:], ACT.Exp, scale=-0.5).then_inc(ev("ro_ready"), 1)
                act.wait_ge(ev("oy_ready"), i + 1)
                A(o_hi[:, i, :], oy[:], ACT.Copy).then_inc(ev("o_hi_ready"), 1)

            act.wait_ge(ev("kes_ready"), 1)
            act.wait_ge(ev("beta_ready"), 1)
            tables("natural_log_exp_and_others")
            qk_norms(0)
            with act.Fori(0, HA - 2) as i:
                delta(i, False)
            delta(HA - 2, False, True)
            delta(HA - 1, True)

            def residual(name, n):
                s = st[name]
                per = s.n // (2 if s.kc == KH else 1)
                tables("natural_log_exp_and_others")

                def body(i, last):
                    for j in range(s.n):
                        end = last and j == s.n - 1
                        if not end:
                            cast_ahead(s, i, j, last)
                        if s.kc == KD or j % 2:
                            m = j if s.kc == KD else j // 2
                            act.wait_ge(acc_free, s.number(i, j) + 1)
                            A(tmp[:, m % 2, :], h[:, i * per + m, :], ACT.Square).then_inc(ev("h_squared"), 1)
                        if end:
                            cast_ahead(s, i, j, last)
                each(act, s.bodies, body)

            def ffn(layer, n):
                s = st[f"up{layer}"]
                w = vec[:, V_FCONV + 132 * layer:V_FCONV + 132 * layer + 132].rearrange("p (g f t) -> p g f t", g=2, t=3)
                wb = vec[:, V_FBIAS + 44 * layer:V_FBIAS + 44 * layer + 44].rearrange("p (g f a) -> p g f a", g=2, a=1)
                tables("silu_and_others")

                def body(i, last):
                    for j in range(4):
                        f, g = i * 2 + j // 2, j % 2
                        cast_ahead(s, i, j, last)
                        A(fy[:, j, :], acc[:, j % 2, :], ACT.Identity, scale=w[:, g, f, 2:3], bias=wb[:, g, f, :]
                          ).then_inc(ev("ffn_newest"), 1)
                        if g == 1:
                            act.wait_ge(acc_free, s.number(i, j - 1) + 1)
                            A(fy[:, j - 1, :], fy[:, j - 1, :], ACT.Silu).then_inc(ev("gate_silu"), 1)
                            act.wait_ge(ev("hid_ready"), f + (KF * layer + 1))
                            A(hid_hi[:, f, :], fy[:, j, :], ACT.Copy).then_inc(ev("hid_hi_ready"), 1)
                each(act, s.bodies, body)
                residual(f"down{layer}", n)

            def attention():
                s = st["attn"]

                for j in range(3):
                    cast_ahead(s, 0, j, False)

                def copy_kv(i):
                    act.wait_ge(acc_done, s.number(i, 1) + 1)
                    A(at_k[:], acc[:, 0, :], ACT.Copy).then_inc(acc_free, 1)
                    A(at_v[:], acc[:, 1, :], ACT.Copy).then_inc(acc_free, 1)

                def copy_q(i):
                    act.wait_ge(acc_done, s.number(i, 2) + 1)
                    A(at_q[:], acc[:, 2, :], ACT.Copy, scale=0.125).then_inc(acc_free, 1)

                copy_kv(0)
                copy_q(0)

                def body(i, more):
                    act.wait_ge(ev("at_v_turned"), i + 1)
                    A(at_vt[:].rearrange("p t q -> p (t q)"), pb[:], ACT.Copy).then_inc(ev("at_vt_ready"), 1)
                    for step in range(8 + 2):
                        if more and step in (4, 8):
                            cast_ahead(s, i + 1, step // 4 - 1, more == 1)
                        if more and step == 8:
                            act.wait_ge(ev("scores_done"), i * 8 + 8)
                            copy_kv(i + 1)
                        if step < 8:
                            u, w = step, (step % 4 + 1) * P
                            act.wait_ge(ev("scored"), i * 8 + (u + 1))
                            A(prob[:, u % 4, 0:w], prob[:, u % 4, 0:w], ACT.Exp, bias=nmax[:, u:u + 1],
                              accum_out=psum_[:, u:u + 1]).then_inc(ev("prob_exp"), 1)
                        if step >= 2:
                            u, w = step - 2, ((step - 2) % 4 + 1) * P
                            act.wait_ge(ev("prob_turned"), i * 8 + (u + 1))
                            if u >= 2:
                                act.wait_ge(ev("pv_done"), i * 8 + (u - 1))
                            A(probT[:, u % 2, 0:w], [pb, pc][u % 2][:, 0:w], ACT.Copy).then_inc(ev("probT_ready"), 1)
                    if more:
                        copy_q(i + 1)
                    act.wait_ge(ev("pv_done"), i * 8 + 8)
                    act.wait_ge(ev("ob_lo_ready"), i)
                    A(at_o[:], pd[:], ACT.Copy).then_inc(ev("at_o_read"), 1)
                    act.wait_ge(ev("at_o_read"), i + 1)
                    A(ob_hi[:, i, :], at_o[:], ACT.Copy).then_inc(ev("ob_hi_ready"), 1)
                    if more:
                        cast_ahead(s, i + 1, 2, more == 1)
                each_ahead(act, PAIRS, body)

            def stick():
                s = st["stick"]

                tables("natural_log_exp_and_others")
                for j in range(3):
                    cast_ahead(s, 0, j, False)

                def copy_kv(i):
                    act.wait_ge(acc_done, s.number(i, 1) + 1)
                    A(sk_k[:], acc[:, 0, :], ACT.Copy).then_inc(acc_free, 1)
                    A(sk_v[:], acc[:, 1, :], ACT.Copy).then_inc(acc_free, 1)

                def copy_q(i):
                    act.wait_ge(acc_done, s.number(i, 2) + 1)
                    A(sk_q[:], acc[:, 2, :], ACT.Copy, scale=0.125).then_inc(acc_free, 1)

                copy_kv(0)
                copy_q(0)

                def body(i, more):
                    act.wait_ge(ev("sk_v_turned"), i + 1)
                    A(sk_vt[:].rearrange("p t q -> p (t q)"), pb[:], ACT.Copy).then_inc(ev("sk_vt_ready"), 1)
                    for step in range(8 + 3):
                        if more and step in (3, 7):
                            cast_ahead(s, i + 1, step // 3 - 1, more == 1)
                        if more and step == 8:
                            act.wait_ge(ev("logits_done"), i * 8 + 8)
                            copy_kv(i + 1)
                        if step < 8:
                            u, e, k = step, step // 4, 3 - step % 4
                            g = slice(SEG[k], SEG[k] + (4 - k) * P)
                            act.wait_ge(ev("logits_done"), i * 8 + (u + 1))
                            A(zs[:, e, g], pa[:, u % 2, 0:(4 - k) * P], ACT.Copy).then_inc(ev("zs_ready"), 1)
                        if 1 <= step < 9:
                            u, e, k = step - 1, (step - 1) // 4, 3 - (step - 1) % 4
                            g = slice(SEG[k], SEG[k] + (4 - k) * P)
                            act.wait_ge(ev("z_abs"), i * 8 + (u + 1))
                            A(sw[:, e, g], sw[:, e, g], ACT.Exp, scale=-1.0).then_inc(ev("z_exp"), 1)
                            act.wait_ge(ev("z_exp"), i * 8 + (u + 1))
                            A(sw[:, e, g], sw[:, e, g], ACT.Ln, bias=1.0).then_inc(ev("z_ln"), 1)
                        if step >= 3:
                            u, e, k = step - 3, (step - 3) // 4, 3 - (step - 3) % 4
                            g = slice(SEG[k], SEG[k] + (4 - k) * P)
                            act.wait_ge(ev("dmasked"), i * 8 + (u + 1))
                            A(sw[:, e, g], zs[:, e, g], ACT.Exp).then_inc(ev("sw_ready"), 1)
                    if more:
                        copy_q(i + 1)
                    act.wait_ge(ev("sk_o_ready"), i + 1)
                    A(ya_hi[:, i, :], sk_o[:], ACT.Copy).then_inc(ev("ya_hi_ready"), 1)
                    if more:
                        cast_ahead(s, i + 1, 2, more == 1)
                each_ahead(act, SBP, body)

            def gating():
                s = st["sgu"]

                def body(i, last):
                    tables("gelu_apprx_tanh_and_others")
                    cast_ahead(s, i, 0, last)
                    A(gv[:], acc[:, 0, :], ACT.Gelu_apprx_tanh).then_inc(acc_free, 1)
                    cast_ahead(s, i, 1, last)
                    cast_ahead(s, i, 2, last)
                    act.wait_ge(ev("gy_ready"), i)
                    A(gu[:], acc[:, 1, :], ACT.Gelu_apprx_tanh).then_inc(acc_free, 1)
                    tables("silu_and_others")
                    A(gz[:], acc[:, 2, :], ACT.Silu).then_inc(acc_free, 1)
                    tables("natural_log_exp_and_others")
                    act.wait_ge(ev("var_ready"), i + 1)
                    A(var[:], var[:], ACT.Ln, bias=eps_d, scale=1.0 / 64).then_inc(ev("var_ln"), 1)
                    act.wait_ge(ev("var_ln"), i + 1)
                    A(var[:], var[:], ACT.Exp, scale=-0.5).then_inc(ev("rvar_ready"), 1)
                    act.wait_ge(ev("gy_ready"), i + 1)
                    A(yb_hi[:, i, :], gy[:], ACT.Copy).then_inc(ev("yb_hi_ready"), 1)
                each(act, GPP, body)

            def merge():
                s = st["merge"]
                tables("sigmoid_and_others")

                def body(i, last):
                    act.wait_ge(ev("mg_hi_ready"), i)
                    act.wait_ge(ev("mg_ready"), i)
                    cast_ahead(s, i, 0, last)
                    A(ga[:, 0, :], acc[:, 0, :], ACT.Sigmoid).then_inc(acc_free, 1)
                    cast_ahead(s, i, 1, last)
                    A(ga[:, 1, :], acc[:, 1, :], ACT.Sigmoid).then_inc(acc_free, 1)
                    cast_ahead(s, i, 2, last)
                    act.wait_ge(ev("mg_ready"), i + 1)
                    A(mg_hi[:, i, :], mg[:, 0, :], ACT.Copy).then_inc(ev("mg_hi_ready"), 1)
                each(act, s.bodies, body)

            n = 1
            if "a_out" in stages:
                residual("a_out", n)
            if "up0" in stages:
                root(n)
                cast_x(1, xhi)
                n += 1
                ffn(0, n)
            if "attn" in stages:
                open_stage("attn", (0, 1))
                root(n)
                open_stage("attn", (2,))
                cast_x(2, xhi)
                cast_x(3, xq_hi)
                n += 1
                attention()
            if "b_out" in stages:
                open_stage("b_out")
                residual("b_out", n)
            if "up1" in stages:
                root(n)
                cast_x(4, xhi)
                n += 1
                ffn(1, n)
            if "stick" in stages:
                root(n)
                n += 1
                for k in range(KD):
                    act.wait_ge(ev("h_ready"), k + 1)
                    act.wait_ge(ev("ssq_added"), KD * n + max(k - 3, 0))
                    A(normed(k), h[:, k, :], ACT.Square).then_inc(ev("h_squared"), 1)
                root(n)
                cast_x(5, xhi)
                n += 1
                s = st["stick_z"]
                tables("silu_and_others")
                for j in range(4):
                    cast_ahead(s, 0, j, True)
                    A(sk_z[:, j, :], acc[:, j % 2, :], ACT.Silu).then_inc(acc_free, 1)
                open_stage("stick")
                stick()
            if "sgu" in stages:
                gating()
            if "merge" in stages:
                merge()
            if "out" in stages:
                open_stage("out")
                residual("out", n)
            root(n)

        @block.vector
        def _(dve):
            tt_ = nc.vector.tensor_tensor
            ts_ = nc.vector.tensor_scalar
            stt = nc.vector.scalar_tensor_tensor

            def low(s, i, j):
                dve.wait_ge(w_hi_ready, s.number(i, j) + 1)
                tt_(split(s, j, 1), raw(s, j), split(s, j, 0).bitcast(F32), ALU.subtract).then_inc(w_lo_ready, 1)

            def low_ahead(s, i, j, last):
                if j + s.slots < s.n:
                    low(s, i, j + s.slots)
                elif not last:
                    low(s, i + 1, j + s.slots - s.n)
                elif s.follow:
                    low(s.follow, 0, j + s.slots - s.n)

            def open_stage(name, js=None):
                s = st[name]
                for j in js or range(s.slots):
                    low(s, 0, j)

            def scale_x(n, m, gain, hi, lo):
                dve.wait_ge(ev("rstd_ready"), n + 1)
                for k in range(KD + 2):
                    if k < KD:
                        if m > 0 or k >= 4:
                            dve.wait_ge(ev("x_lo_ready"), KD * m + max(k - 3, 0))
                        stt(normed(k), h[:, k, :], vec[:, gain + k:gain + k + 1], rstd[:], ALU.mult, ALU.mult
                            ).then_inc(ev("xn_ready"), 1)
                    if k >= 2:
                        dve.wait_ge(ev("x_hi_ready"), KD * m + k - 1)
                        tt_(lo[:, k - 2, :], normed(k - 2), hi[:, k - 2, :].bitcast(F32), ALU.subtract
                            ).then_inc(ev("x_lo_ready"), 1)

            def clear_ssq(n):
                nc.vector.memset(ssq[:], 0.0).then_inc(ev("ssq_cleared"), 1)
                dve.wait_ge(ev("ssq_cleared"), n + 1)

            nc.vector.memset(epst[:], EPS).then_inc(ev("eps_ready"), 1)
            clear_ssq(0)
            for k in range(KD):
                dve.wait_ge(ev("h_squared"), k + 1)
                if k > 0:
                    dve.wait_ge(ev("ssq_added"), k)
                tt_(ssq[:], ssq[:], normed(k), ALU.add).then_inc(ev("ssq_added"), 1)
            dve.wait_ge(ev("rel_landed"), 16)
            nc.vector.tensor_copy(ext[:, 0:255], relf[:, 0:1].to_broadcast([2 * PAIRS, 255])).then_inc(ev("ext_ready"), 1)
            nc.vector.tensor_copy(ext[:, 255:EXT], relf[:, 0:EXT - 255]).then_inc(ev("ext_ready"), 1)
            s = st["delta"]
            dve.wait_ge(ev("wg_hi_ready"), 1)
            tt_(wg_lo[:], wg[:], wg_hi[:].bitcast(F32), ALU.subtract).then_inc(ev("wg_lo_ready"), 1)
            low(s, -1, 1)
            low(s, -1, 2)
            dve.wait_ge(ev("consts_landed"), 32)
            scale_x(0, 0, G_A, xhi, xlo)

            gates = pb[:, 0:64].rearrange("p (t c) -> p c t", c=16)
            hc = [P, HA, NC]
            dve.wait_ge(ev("beta_exp"), 1)
            ts_(beta[:], t0[:], 1.0, None, ALU.add).then_inc(ev("gate_step"), 1)
            dve.wait_ge(ev("gate_step"), 1)
            nc.vector.reciprocal(beta[:], beta[:]).then_inc(ev("beta_ready"), 1)
            dve.wait_ge(ev("gates_landed"), 48)
            tt_(gg[:], gates[:, 8:16, :], dtb[:].unsqueeze(2).to_broadcast(hc), ALU.add).then_inc(ev("gate_step"), 1)
            dve.wait_ge(ev("gate_step"), 2)
            stt(t1[:], gg[:], -1.0, gg[:], ALU.mult, ALU.max).then_inc(ev("gate_abs"), 1)
            dve.wait_ge(ev("gate_ln"), 1)
            stt(gg[:], gg[:], 0.0, t1[:], ALU.max, ALU.add).then_inc(ev("gate_step"), 1)
            dve.wait_ge(ev("gate_step"), 3)
            dve.wait_ge(ev("alog_exp"), 1)
            stt(gg[:], gg[:], -1.0, alog[:].unsqueeze(2).to_broadcast(hc), ALU.mult, ALU.mult).then_inc(ev("gg_ready"), 1)

            def conv_older(i, j, head, taps=(1, 2, 3)):
                w = vec[:, V_ACONV + 32 * (j - 1):V_ACONV + 32 * j].rearrange("p (h t) -> p h t", t=4)
                if 1 in taps:
                    dve.wait_ge(ev("conv_newest"), i * 3 + (3 + j))
                for d in taps:
                    if d > 1:
                        dve.wait_ge(ev("conv_tap"), i * 6 + (6 + 2 * (j - 1) + d - 1))
                    x = stt(ys[:, j - 1, d:S], acc[:, j % 2, 0:S - d], w[:, head, 3 - d:4 - d], ys[:, j - 1, d:S],
                            ALU.mult, ALU.add)
                    x.then_inc(ev("conv_tap") if d < 3 else acc_free, 1)

            low(s, -1, 3)
            conv_older(-1, 1, 0)
            low(s, 0, 0)
            conv_older(-1, 2, 0)
            low(s, 0, 1)
            conv_older(-1, 3, 0)

            dve.wait_ge(ev("cum_done"), 1)
            flat = lambda t: t[:].rearrange("p h t -> p (h t)")
            nc.vector.tensor_copy(flat(cc), pb[:, 0:32]).then_inc(ev("cc_ready"), 1)
            dve.wait_ge(ev("cc_ready"), 1)
            dve.wait_ge(ev("beta_ready"), 1)
            tt_(flat(kes), pb[:, 32:64], flat(cc), ALU.subtract).then_inc(ev("kes_diff"), 1)
            dve.wait_ge(ev("rows_turned"), 1)
            nc.vector.tensor_copy(rows[:].rearrange("r a p -> r (a p)"), pc[0:32, 0:2 * P]).then_inc(ev("rows_ready"), 1)
            dve.wait_ge(ev("nbe_exp"), 1)
            stt(nbe[:], nbe[:], -1.0, beta[:], ALU.mult, ALU.mult).then_inc(ev("nbe_ready"), 1)

            NL = len(LEVELS)

            def unit_qk(i):
                dve.wait_ge(ev("rqk_ready"), i + 1)
                tt_(kn[:], ys[:, 1, :], rqk[:, 1, :], ALU.mult).then_inc(ev("kn_ready"), 1)
                stt(kq[:, :, 1, :], chunks(ys[:, 0, :]), float(P) ** -0.5, chunks(rqk[:, 0, :]), ALU.mult, ALU.mult
                    ).then_inc(ev("qn_ready"), 1)
                dve.wait_ge(ev("kn_ready"), i + 1)
                dve.wait_ge(ev("brow_landed"), i * 16 + 16)
                tt_(kq[:, :, 0, :], chunks(kn[:]), chunks(brow[:]), ALU.mult).then_inc(ev("kb_ready"), 1)

            def delta(i, last, last_qkv=False):
                def between(gap):
                    if last:
                        return
                    if gap in (0, 1, 2):
                        conv_older(i, 1, i + 1, (gap + 1,))
                    if gap == 6:
                        low(s, i + 1, 0)
                    if gap in (7, 8, 9):
                        conv_older(i, 2, i + 1, (gap - 6,))
                    if gap in (11, 12, 13):
                        conv_older(i, 3, i + 1, (gap - 10,))
                    if gap == 14 and not last_qkv:
                        low(s, i + 1, 1)

                dve.wait_ge(ev("qn_ready"), i + 1)
                dve.wait_ge(ev("ecrow_ready"), i + 1)
                tt_(chunks(qe[:]), kq[:, :, 1, :], chunks(ecrow[:]), ALU.mult)
                for t in range(NC):
                    x = ts_(dec[:, t, :], crow[:, t * P:t * P + P], cc[:, i, t:t + 1], 0.0, ALU.subtract, ALU.min)
                x.then_inc(ev("dec_exponent"), 1)
                if not last:
                    low(s, i, 2)
                dve.wait_ge(ev("dec_ready"), i + 1)
                tt_(gd[:], dec[:].unsqueeze(2).to_broadcast([P, NC, 2, P]),
                    cst[:, C_INCL2:C_INCL2 + 2, :].unsqueeze(1).to_broadcast([P, NC, 2, P]), ALU.mult
                    ).then_inc(ev("decay_masked"), 1)
                dve.wait_ge(ev("decay_masked"), i + 1)
                dve.wait_ge(ev("gram_done"), i + 1)
                tt_(gd[:].rearrange("p t a q -> p (t a q)"), pa[:].rearrange("p a q -> p (a q)"),
                    gd[:].rearrange("p t a q -> p (t a q)"), ALU.mult).then_inc(ev("gd_ready"), 1)
                dve.wait_ge(ev("gd_ready"), i + 1)
                tt_(tt[:], gd[:, :, 0, :], over_chunks(cst[:, C_M1, :]), ALU.mult).then_inc(ev("m1_ready"), 1)
                dve.wait_ge(ev("m1_ready"), i + 1)
                tt_(tt[:], tt[:], over_chunks(ident), ALU.add).then_inc(ev("tt_ready"), 1)
                dve.wait_ge(ev("tn_turned"), i + 1)
                nc.vector.tensor_copy(tn[:], chunks(pd[:])).then_inc(ev("tn_ready"), 1)
                if last:
                    open_stage("a_out")
                else:
                    low(s, i, 3)
                for n in range(NL):
                    dve.wait_ge(ev("x_done"), i * NL + (n + 1))
                    tt_(xm[:], chunks(pb[:]), over_chunks(cst[:, C_LEV + n, :]), ALU.mult).then_inc(ev("xm_ready"), 1)
                    between(2 * n)
                    if n < NL - 1:
                        dve.wait_ge(ev("join_done"), i * (2 * NL - 1) + (2 * n + 1))
                        tt_(tn[:], tn[:], chunks(pc[:]), ALU.add).then_inc(ev("tn_ready"), 1)
                    dve.wait_ge(ev("join_done"), i * (2 * NL - 1) + min(2 * n + 2, 2 * NL - 1))
                    dve.wait_ge(ev("tt_ready"), i * (NL + 1) + (n + 1))
                    tt_(tt[:], tt[:], chunks(pd[:]), ALU.add).then_inc(ev("tt_ready"), 1)
                    between(2 * n + 1)
                for t in range(NC):
                    q = slice(t * P, t * P + P)
                    if t > 0:
                        dve.wait_ge(ev("ks_done"), i * (NC - 1) + t)
                        stt(rr[:, t, :], pb[:, q], nbe[:, i, t:t + 1], bv[:, t, :], ALU.mult, ALU.add
                            ).then_inc(ev("r_ready"), 1)
                    if t < NC - 1:
                        dve.wait_ge(ev("s_done"), i * (NC - 1) + (t + 1))
                        if t == 0:
                            nc.vector.tensor_copy(state[:], pd[:, q]).then_inc(ev("state_ready"), 1)
                        else:
                            dve.wait_ge(ev("state_ready"), i * (NC - 1) + t)
                            stt(state[:], state[:], ecl[:, i, t:t + 1], pd[:, q], ALU.mult, ALU.add
                                ).then_inc(ev("state_ready"), 1)
                        between(2 * NL + t)
                if not last:
                    unit_qk(i + 1)
                dve.wait_ge(ev("ro_ready"), i + 1)
                stt(oy[:], osb[:], vec[:, V_AOUT:V_AOUT + 1], ro[:], ALU.mult, ALU.mult).then_inc(ev("on_ready"), 1)
                dve.wait_ge(ev("on_ready"), i + 1)
                dve.wait_ge(ev("z_silu"), i + 1)
                tt_(oy[:], oy[:], ys[:, 3, :], ALU.mult).then_inc(ev("oy_ready"), 1)
                dve.wait_ge(ev("o_hi_ready"), i + 1)
                tt_(o_lo[:, i, :], oy[:], o_hi[:, i, :].bitcast(F32), ALU.subtract).then_inc(ev("o_lo_ready"), 1)

            dve.wait_ge(ev("bias_table"), 48)
            dve.wait_ge(ev("nbe_ready"), 1)
            dve.wait_ge(ev("ecl_ready"), 1)
            unit_qk(0)
            with dve.Fori(0, HA - 2) as i:
                delta(i, False)
            delta(HA - 2, False, True)
            delta(HA - 1, True)

            def residual(name, n):
                s = st[name]
                per = s.n // (2 if s.kc == KH else 1)
                clear_ssq(n)

                def body(i, last):
                    for j in range(s.n):
                        m = j if s.kc == KD else j // 2
                        if s.kc == KD or j % 2:
                            dve.wait_ge(acc_done, s.number(i, j) + 1)
                            tt_(h[:, i * per + m, :], h[:, i * per + m, :], acc[:, m % 2, :], ALU.add
                                ).then_inc(acc_free, 1 if s.kc == KD else 2)
                        end = last and j == s.n - 1
                        if not end:
                            low_ahead(s, i, j, last)
                        if s.kc == KD or j % 2:
                            dve.wait_ge(ev("h_squared"), i * per + (KD * n + m + 1))
                            dve.wait_ge(ev("ssq_added"), i * per + (KD * n + m))
                            tt_(ssq[:], ssq[:], tmp[:, m % 2, :], ALU.add).then_inc(ev("ssq_added"), 1)
                        if end:
                            low_ahead(s, i, j, last)
                each(dve, s.bodies, body)

            def ffn(layer, n):
                s = st[f"up{layer}"]
                w = vec[:, V_FCONV + 132 * layer:V_FCONV + 132 * layer + 132].rearrange("p (g f t) -> p g f t", g=2, t=3)

                def body(i, last):
                    for j in range(4):
                        f, g = i * 2 + j // 2, j % 2
                        low_ahead(s, i, j, last)
                        dve.wait_ge(ev("ffn_newest"), i * 4 + (2 * KF * layer + j + 1))
                        stt(fy[:, j, 1:S], acc[:, j % 2, 0:S - 1], w[:, g, f, 1:2], fy[:, j, 1:S], ALU.mult, ALU.add
                            ).then_inc(ev("ffn_tap"), 1)
                        dve.wait_ge(ev("ffn_tap"), i * 4 + (2 * KF * layer + j + 1))
                        stt(fy[:, j, 2:S], acc[:, j % 2, 0:S - 2], w[:, g, f, 0:1], fy[:, j, 2:S], ALU.mult, ALU.add
                            ).then_inc(acc_free, 1)
                        if g == 1:
                            dve.wait_ge(ev("gate_silu"), f + (KF * layer + 1))
                            dve.wait_ge(acc_free, s.number(i, j) + 1)
                            tt_(fy[:, j, :], fy[:, j, :], fy[:, j - 1, :], ALU.mult).then_inc(ev("hid_ready"), 1)
                            dve.wait_ge(ev("hid_hi_ready"), f + (KF * layer + 1))
                            tt_(hid_lo[:, f, :], fy[:, j, :], hid_hi[:, f, :].bitcast(F32), ALU.subtract
                                ).then_inc(ev("hid_lo_ready"), 1)
                each(dve, s.bodies, body)
                residual(f"down{layer}", n)

            def attention():
                s = st["attn"]

                for j in range(3):
                    low_ahead(s, 0, j, False)

                def body(i, more):
                    dve.wait_ge(ev("bias_landed"), i * 16 + 16)
                    for step in range(8 + 1):
                        if more and step in (4, 8):
                            low_ahead(s, i + 1, step // 4 - 1, more == 1)
                        if step < 8:
                            u, e, b = step, step // 4, step % 4
                            w = (b + 1) * P
                            dve.wait_ge(ev("scores_done"), i * 8 + (u + 1))
                            if u >= 4:
                                dve.wait_ge(ev("prob_turned"), i * 8 + (u - 3))
                            tt_(prob[:, u % 4, 0:w], pa[:, u % 2, 0:w], bias[:, e, S - w:S], ALU.add
                                ).then_inc(ev("biased"), 1)
                            dve.wait_ge(ev("biased"), i * 8 + (u + 1))
                            nc.vector.tensor_reduce(nmax[:, u:u + 1], prob[:, u % 4, 0:w], AX_X, ALU.max, negate=True
                                                    ).then_inc(ev("scored"), 1)
                        if step >= 1:
                            u, w = step - 1, ((step - 1) % 4 + 1) * P
                            dve.wait_ge(ev("prob_exp"), i * 8 + (u + 1))
                            nc.vector.reciprocal(psum_[:, u:u + 1], psum_[:, u:u + 1]).then_inc(ev("prob_rsum"), 1)
                            dve.wait_ge(ev("prob_rsum"), i * 8 + (u + 1))
                            ts_(prob[:, u % 4, 0:w], prob[:, u % 4, 0:w], psum_[:, u:u + 1], None, ALU.mult
                                ).then_inc(ev("prob_ready"), 1)
                    dve.wait_ge(ev("ob_hi_ready"), i + 1)
                    tt_(ob_lo[:, i, :], at_o[:], ob_hi[:, i, :].bitcast(F32), ALU.subtract).then_inc(ev("ob_lo_ready"), 1)
                    if more:
                        low_ahead(s, i + 1, 2, more == 1)
                each_ahead(dve, PAIRS, body)

            def stick():
                s = st["stick"]

                for j in range(3):
                    low_ahead(s, 0, j, False)

                def body(i, more):
                    for step in range(8 + 3):
                        if more and step in (4, 7):
                            low_ahead(s, i + 1, step // 3 - 1, more == 1)
                        if step < 8:
                            u, e, k = step, step // 4, 3 - step % 4
                            g = slice(SEG[k], SEG[k] + (4 - k) * P)
                            dve.wait_ge(ev("zs_ready"), i * 8 + (u + 1))
                            stt(sw[:, e, g], zs[:, e, g], -1.0, zs[:, e, g], ALU.mult, ALU.max).then_inc(ev("z_abs"), 1)
                        if 1 <= step < 9:
                            u, e, k = step - 1, (step - 1) // 4, 3 - (step - 1) % 4
                            g = slice(SEG[k], SEG[k] + (4 - k) * P)
                            dve.wait_ge(ev("z_ln"), i * 8 + (u + 1))
                            stt(sp[:, e, g], zs[:, e, g], 0.0, sw[:, e, g], ALU.max, ALU.add).then_inc(ev("sp_whole"), 1)
                            dve.wait_ge(ev("sp_whole"), i * 8 + (u + 1))
                            tt_(sp[:, e, SEG[k]:SEG[k] + P], sp[:, e, SEG[k]:SEG[k] + P], cst[:, C_INCL2, :], ALU.mult
                                ).then_inc(ev("sp_ready"), 1)
                        if step >= 3:
                            u, e, k = step - 3, (step - 3) // 4, 3 - (step - 3) % 4
                            g = slice(SEG[k], SEG[k] + (4 - k) * P)
                            dve.wait_ge(ev("suffix_done"), i * 8 + (u + 1))
                            tt_(zs[:, e, g], zs[:, e, g], [pb, pc][u % 2][:, 0:(4 - k) * P], ALU.subtract
                                ).then_inc(ev("drest"), 1)
                            dve.wait_ge(ev("drest"), i * 8 + (u + 1))
                            tt_(zs[:, e, SEG[k]:SEG[k] + P], zs[:, e, SEG[k]:SEG[k] + P], cst[:, C_NEGD, :], ALU.add
                                ).then_inc(ev("dmasked"), 1)
                    dve.wait_ge(ev("sk_o_done"), i + 1)
                    tt_(sk_o[:], pd[:], sk_z[:, i, :], ALU.mult).then_inc(ev("sk_o_ready"), 1)
                    dve.wait_ge(ev("ya_hi_ready"), i + 1)
                    tt_(ya_lo[:, i, :], sk_o[:], ya_hi[:, i, :].bitcast(F32), ALU.subtract).then_inc(ev("ya_lo_ready"), 1)
                    if more:
                        low_ahead(s, i + 1, 2, more == 1)
                each_ahead(dve, SBP, body)

            def gating():
                s = st["sgu"]

                def body(i, last):
                    for j in range(3):
                        low_ahead(s, i, j, last)
                    g8 = [P, 2 * NC, 64]
                    turned = pb[:].rearrange("p (g c) -> p g c", c=64)
                    dve.wait_ge(ev("gv_turned"), i + 1)
                    nc.vector.tensor_reduce(mu[:], turned, AX_X, ALU.add).then_inc(ev("vnorm_step"), 1)
                    dve.wait_ge(ev("vnorm_step"), i * 6 + 1)
                    ts_(mu[:], mu[:], 1.0 / 64, None, ALU.mult).then_inc(ev("vnorm_step"), 1)
                    dve.wait_ge(ev("vnorm_step"), i * 6 + 2)
                    tt_(xc[:], turned, mu[:].unsqueeze(2).to_broadcast(g8), ALU.subtract).then_inc(ev("vnorm_step"), 1)
                    dve.wait_ge(ev("vnorm_step"), i * 6 + 3)
                    tt_(xs2[:], xc[:], xc[:], ALU.mult).then_inc(ev("vnorm_step"), 1)
                    dve.wait_ge(ev("vnorm_step"), i * 6 + 4)
                    nc.vector.tensor_reduce(var[:], xs2[:], AX_X, ALU.add).then_inc(ev("var_ready"), 1)
                    dve.wait_ge(ev("rvar_ready"), i + 1)
                    tt_(xc[:], xc[:], var[:].unsqueeze(2).to_broadcast(g8), ALU.mult).then_inc(ev("vnorm_step"), 1)
                    dve.wait_ge(ev("lngb_landed"), 16)
                    x4 = xc[:].rearrange("p (t e) c -> p t (e c)", e=2)
                    dve.wait_ge(ev("vnorm_step"), i * 6 + 5)
                    tt_(x4, x4, over_chunks(lngb[:, 0, i, :]), ALU.mult).then_inc(ev("vnorm_step"), 1)
                    dve.wait_ge(ev("vnorm_step"), i * 6 + 6)
                    tt_(x4, x4, over_chunks(lngb[:, 1, i, :]), ALU.add).then_inc(ev("vn_spatial_ready"), 1)
                    dve.wait_ge(acc_free, s.number(i, 2) + 1)
                    tt_(gu[:], gu[:], gz[:], ALU.mult).then_inc(ev("uz_ready"), 1)
                    dve.wait_ge(ev("mixed"), i + 1)
                    dve.wait_ge(ev("bsp_landed"), 32)
                    tt_(chunks(gy[:]), chunks(pc[:]), over_chunks(bsp[:, i, :]), ALU.add).then_inc(ev("mixed_read"), 1)
                    dve.wait_ge(ev("mixed_read"), i + 1)
                    dve.wait_ge(ev("uz_ready"), i + 1)
                    tt_(gy[:], gy[:], gu[:], ALU.mult).then_inc(ev("gy_ready"), 1)
                    dve.wait_ge(ev("yb_hi_ready"), i + 1)
                    tt_(yb_lo[:, i, :], gy[:], yb_hi[:, i, :].bitcast(F32), ALU.subtract).then_inc(ev("yb_lo_ready"), 1)
                each(dve, GPP, body)

            def merge():
                s = st["merge"]

                def body(i, last):
                    low_ahead(s, i, 0, last)
                    low_ahead(s, i, 1, last)
                    dve.wait_ge(acc_done, s.number(i, 2) + 1)
                    dve.wait_ge(acc_free, s.number(i, 1) + 1)
                    dve.wait_ge(ev("mg_lo_ready"), i)
                    tt_(mg[:, 1, :], pa[:, 0, :], ga[:, 1, :], ALU.mult).then_inc(ev("mg_b"), 1)
                    tt_(mg[:, 0, :], acc[:, 2, :], ga[:, 0, :], ALU.mult).then_inc(acc_free, 1)
                    dve.wait_ge(ev("mg_b"), i + 1)
                    dve.wait_ge(acc_free, s.number(i, 2) + 1)
                    tt_(mg[:, 0, :], mg[:, 0, :], mg[:, 1, :], ALU.add).then_inc(ev("mg_ready"), 1)
                    low_ahead(s, i, 2, last)
                    dve.wait_ge(ev("mg_hi_ready"), i + 1)
                    dve.wait_ge(ev("mg_ready"), i + 1)
                    tt_(mg_lo[:, i, :], mg[:, 0, :], mg_hi[:, i, :].bitcast(F32), ALU.subtract).then_inc(ev("mg_lo_ready"), 1)
                each(dve, s.bodies, body)

            n = 1
            if "a_out" in stages:
                residual("a_out", n)
            if "up0" in stages:
                scale_x(n, 1, G_F, xhi, xlo)
                n += 1
                ffn(0, n)
            if "attn" in stages:
                open_stage("attn", (0, 1))
                scale_x(n, 2, G_KV, xhi, xlo)
                open_stage("attn", (2,))
                scale_x(n, 3, G_B, xq_hi, xq_lo)
                n += 1
                attention()
            if "b_out" in stages:
                open_stage("b_out")
                residual("b_out", n)
            if "up1" in stages:
                scale_x(n, 4, G_F + 8, xhi, xlo)
                n += 1
                ffn(1, n)
            if "stick" in stages:
                dve.wait_ge(ev("rstd_ready"), n + 1)
                n += 1
                clear_ssq(n)
                for k in range(KD + 2):
                    if k < KD:
                        stt(h[:, k, :], h[:, k, :], vec[:, G_FIN + k:G_FIN + k + 1], rstd[:], ALU.mult, ALU.mult
                            ).then_inc(ev("h_ready"), 1)
                    if k >= 2:
                        dve.wait_ge(ev("h_squared"), KD * n + k - 1)
                        dve.wait_ge(ev("ssq_added"), KD * n + k - 2)
                        tt_(ssq[:], ssq[:], normed(k - 2), ALU.add).then_inc(ev("ssq_added"), 1)
                scale_x(n, 5, G_2, xhi, xlo)
                n += 1
                s = st["stick_z"]
                for j in range(4):
                    low_ahead(s, 0, j, True)
                open_stage("stick")
                stick()
            if "sgu" in stages:
                gating()
            if "merge" in stages:
                merge()
            if "out" in stages:
                open_stage("out")
                residual("out", n)
            dve.wait_ge(ev("rstd_ready"), n + 1)
            with dve.Fori(0, KD) as k:
                stt(h[:, k, :], h[:, k, :], vec[:, G_FIN2:G_FIN2 + KD].rearrange("p (k a) -> p k a", a=1)[:, k, :],
                    rstd[:], ALU.mult, ALU.mult).then_inc(ev("final_ready"), 1)


def _constants(np):
    c = np.zeros((P, NCONST, P), np.float32)
    row, col = np.arange(P)[:, None], np.arange(P)[None, :]
    c[:, C_ID] = row == col
    c[:, C_ONE] = 1.0
    c[:, C_CUM] = row <= col
    c[:, C_SUF] = row >= col
    c[:, C_M1] = np.where((col % 2 == 1) & (row == col - 1), -1.0, 0.0)
    c[:, C_INCL2] = row < col
    c[:, C_INCL2 + 1] = row <= col
    c[:, C_NEGD] = np.where(row >= col, NEG, 0.0)
    for n, b in enumerate(LEVELS):
        c[:, C_LEV + n] = np.where(((row // b) % 2 == 1) & (col // b == row // b - 1), -1.0, 0.0)
    return c


def _tiles(np, w):
    k, n = w.shape
    return w.reshape(k // P, P, n // P, P).transpose(2, 1, 0, 3)


def kernel(**inputs):
    import numpy as _np
    import concourse.bacc as _bacc
    from concourse import mybir as _mybir
    from concourse.bass_utils import run_bass_kernel_spmd as _run

    a = {k: _np.asarray(v) for k, v in inputs.items()}
    cat, stack = _np.concatenate, _np.stack

    w = _tiles(_np, a["a_w_in"][0][:, :4 * D])
    order = [w[[0, HA, 2 * HA]]]
    for i in range(HA):
        order.append(w[[3 * HA + i] + ([i + 1, HA + i + 1, 2 * HA + i + 1] if i < HA - 1 else [])])
    order.append(_tiles(_np, a["a_w_out"][0]))

    def up(layer):
        t = _tiles(_np, a["f_w_up"][layer])
        return stack([t[:KF], t[KF:]], 1).reshape(2 * KF, P, KD, P)

    order.append(up(0))
    kv, q = _tiles(_np, a["w_kv"]), _tiles(_np, a["b_w_q"][0])
    order.append(stack([kv[:PAIRS], kv[PAIRS:], q], 1).reshape(3 * PAIRS, P, KD, P))
    order.append(_tiles(_np, a["b_w_out"][0]))
    order.append(up(1))
    w = _tiles(_np, a["w_in_2"][0])
    order.append(w[12:16])
    for i in range(SBP):
        order.append(w[[4 + i, 8 + i, i]])
    for i in range(GPP):
        order.append(w[[20 + i, 16 + i, 24 + i]])
    both = cat([_tiles(_np, a["w_up_a_2"][0]), _tiles(_np, a["w_up_b_2"][0])], 2)
    for i in range(KD):
        order.append(cat([w[[28 + i, 36 + i]], both[i:i + 1]], 0))
    order.append(_tiles(_np, a["w_out_2"][0]))
    w8 = cat(order, 0).reshape(-1, P, KD * P)

    down = [_tiles(_np, a["f_w_down"][n]).reshape(KD, P, 2, KH, P).transpose(0, 2, 1, 3, 4) for n in range(2)]
    w11 = cat(down, 0).reshape(-1, P, KH * P)

    cols = lambda v: v.reshape(-1, P).T
    gains = [a["a_norm"][0], a["kv_norm"], a["b_norm"][0], a["f_norm"][0], a["f_norm"][1], a["final_norm"],
             a["norm_g_2"][0], a["final_norm_g_2"]]
    vecs = [cols(g) for g in gains]
    vecs.append(a["a_conv"][0].reshape(4, 3 * HA, P).transpose(2, 1, 0).reshape(P, -1))
    vecs.append(a["f_conv"].reshape(2, 3, 2 * KF, P).transpose(3, 0, 2, 1).reshape(P, -1))
    vecs.append(a["f_conv_b"].reshape(2, 2 * KF, P).transpose(2, 0, 1).reshape(P, -1))
    vecs.append(a["a_out_norm"][0].reshape(P, 1))

    arrays = {
        "xT": a["x"][0].T.reshape(KD, P, S).transpose(1, 0, 2),
        "w8": w8,
        "w11": w11,
        "w_gates": a["a_w_in"][0][:, 4 * D:].reshape(KD, P, 2 * HA).transpose(1, 0, 2),
        "consts": _constants(_np),
        "vecs": cat(vecs, 1),
        "a_log": a["a_A_log"][0],
        "dt_bias": a["a_dt_bias"][0],
        "rel_flip": a["b_rel_bias"][0][:, ::-1],
        "ln_gb": stack([a["sgu_ln_g_2"][0], a["sgu_ln_b_2"][0]]).reshape(2, GPP, P),
        "w_spat": a["w_spatial_2"][0].transpose(2, 0, 1),
        "b_spat": a["b_spatial_2"][0],
    }
    nc = _bacc.Bacc("TRN2", target_bir_lowering=False, num_devices=1)
    arrays = {k: _np.ascontiguousarray(v) for k, v in arrays.items()}
    args = [nc.dram_tensor(k, v.shape, _mybir.dt.from_np(v.dtype), kind="ExternalInput").ap() for k, v in arrays.items()]
    args.append(nc.dram_tensor("outT", [P, KD, S], F32, kind="ExternalOutput").ap())
    build(nc, *args)
    r = _run(nc, [arrays], core_ids=[0])
    return _np.ascontiguousarray(r.results[0]["outT"].transpose(2, 1, 0)).reshape(1, S, D)
```
